# Optimizing a Trainium2 kernel written in Bass

```python
import jax, jax.numpy as jnp
from jax import lax
import numpy as np
import math

D_MODEL = 1024
BATCH = 1
SEQ = 256
DEPTH = 1

CHUNK = 64
N_PAST_CHUNKS = 8
BAND = (N_PAST_CHUNKS + 1) * CHUNK
ATT_HEADS = 8
ATT_HEAD_DIM = 64
ATT_WIDTH = ATT_HEADS * ATT_HEAD_DIM
MAX_REL = 256
N_REL = 2 * MAX_REL + 1
DN_HEADS = 4
DN_HEAD_DIM = 128
DN_WIDTH = DN_HEADS * DN_HEAD_DIM
CONV_K = 4
D_FF = 4 * D_MODEL
EPS = 1e-6
SPLITS = [ATT_WIDTH, 2 * ATT_WIDTH, 3 * ATT_WIDTH,
          3 * ATT_WIDTH + 3 * DN_WIDTH,
          3 * ATT_WIDTH + 4 * DN_WIDTH,
          3 * ATT_WIDTH + 4 * DN_WIDTH + DN_HEADS]
IN_COLS = 3 * ATT_WIDTH + 4 * DN_WIDTH + 2 * DN_HEADS


def rms_norm(x, g):
    xf = x.astype(jnp.float32)
    y = xf * lax.rsqrt(jnp.mean(xf * xf, axis=-1, keepdims=True) + EPS)
    return (y * g.astype(jnp.float32)).astype(x.dtype)

def l2_norm(x):
    xf = x.astype(jnp.float32)
    return xf * lax.rsqrt(jnp.sum(xf * xf, axis=-1, keepdims=True) + EPS)

def chunked_rel_attention(q, k, v, q_gain, k_gain, rel_bias):
    B, L, H, Dh = q.shape
    nc = L // CHUNK
    q = rms_norm(q, q_gain)
    k = rms_norm(k, k_gain)
    qc = q.reshape(B, nc, CHUNK, H, Dh)
    pad = ((0, 0), (N_PAST_CHUNKS * CHUNK, 0), (0, 0), (0, 0))
    kp = jnp.pad(k, pad).reshape(B, nc + N_PAST_CHUNKS, CHUNK, H, Dh)
    vp = jnp.pad(v, pad).reshape(B, nc + N_PAST_CHUNKS, CHUNK, H, Dh)
    kb = jnp.concatenate([kp[:, j:j + nc] for j in range(N_PAST_CHUNKS + 1)], axis=2)
    vb = jnp.concatenate([vp[:, j:j + nc] for j in range(N_PAST_CHUNKS + 1)], axis=2)
    scores = jnp.einsum('bcqhd,bckhd->bchqk', qc, kb,
                        preferred_element_type=jnp.float32) * (Dh ** -0.5)
    q_pos = N_PAST_CHUNKS * CHUNK + np.arange(CHUNK)
    k_pos = np.arange(BAND)
    rel_idx = np.clip(q_pos[:, None] - k_pos[None, :], -MAX_REL, MAX_REL) + MAX_REL
    bias = rel_bias.astype(jnp.float32)[:, rel_idx]
    scores = scores + bias[None, None]
    key_chunk = jnp.arange(nc)[:, None] + jnp.asarray(k_pos // CHUNK)[None, :] - N_PAST_CHUNKS
    valid = key_chunk >= 0
    scores = jnp.where(valid[None, :, None, None, :], scores, jnp.finfo(jnp.float32).min)
    p = jax.nn.softmax(scores, axis=-1).astype(v.dtype)
    o = jnp.einsum('bchqk,bckhd->bcqhd', p, vb)
    return o.reshape(B, L, H * Dh)

def causal_short_conv(x, w):
    L = x.shape[1]
    xp = jnp.pad(x, ((0, 0), (CONV_K - 1, 0), (0, 0)))
    y = xp[:, 0:L] * w[0]
    for j in range(1, CONV_K):
        y = y + xp[:, j:j + L] * w[j]
    return jax.nn.silu(y)

def gated_delta_rule(q, k, v, g, beta):
    B, L, H, Dk = q.shape
    Dv = v.shape[-1]
    nc = L // CHUNK
    f32 = jnp.float32
    q = l2_norm(q) * (Dk ** -0.5)
    k = l2_norm(k)
    v = v.astype(f32)

    def to_chunks(t):
        return jnp.transpose(t.reshape(B, nc, CHUNK, H, -1), (0, 3, 1, 2, 4))

    q, k, v = to_chunks(q), to_chunks(k), to_chunks(v)
    g = jnp.transpose(g.astype(f32).reshape(B, nc, CHUNK, H), (0, 3, 1, 2))
    beta = jnp.transpose(beta.astype(f32).reshape(B, nc, CHUNK, H), (0, 3, 1, 2))
    decay = jnp.cumsum(g, axis=-1)
    tril = jnp.asarray(np.tril(np.ones((CHUNK, CHUNK), dtype=bool)))
    strict = jnp.asarray(np.tril(np.ones((CHUNK, CHUNK), dtype=bool), -1))
    diff = decay[..., :, None] - decay[..., None, :]
    l_mask = jnp.where(tril, jnp.exp(jnp.where(tril, diff, 0.0)), 0.0)
    k_beta = k * beta[..., None]
    v_beta = v * beta[..., None]
    a_strict = jnp.where(strict, jnp.einsum('bhnid,bhnjd->bhnij', k_beta, k) * l_mask, 0.0)
    t_mat = a_strict + jnp.eye(CHUNK, dtype=f32)
    value = lax.linalg.triangular_solve(t_mat, v_beta, left_side=True, lower=True,
                                        unit_diagonal=True)
    k_cumdecay = lax.linalg.triangular_solve(t_mat, k_beta * jnp.exp(decay)[..., None],
                                             left_side=True, lower=True, unit_diagonal=True)
    attn_intra = jnp.where(tril, jnp.einsum('bhnid,bhnjd->bhnij', q, k) * l_mask, 0.0)
    q_decay = q * jnp.exp(decay)[..., None]
    k_tail = k * jnp.exp(decay[..., -1:] - decay)[..., None]
    chunk_decay = jnp.exp(decay[..., -1])

    def step(S, inp):
        qd, kc, val, att, kt, cd = inp
        v_new = val - jnp.einsum('bhcd,bhde->bhce', kc, S)
        o = jnp.einsum('bhcd,bhde->bhce', qd, S) + jnp.einsum('bhij,bhje->bhie', att, v_new)
        S = S * cd[..., None, None] + jnp.einsum('bhcd,bhce->bhde', kt, v_new)
        return S, o

    xs = tuple(jnp.moveaxis(t, 2, 0) for t in
               (q_decay, k_cumdecay, value, attn_intra, k_tail, chunk_decay))
    S0 = jnp.zeros((B, H, Dk, Dv), f32)
    _, o = lax.scan(step, S0, xs)
    return jnp.transpose(o, (1, 0, 3, 2, 4)).reshape(B, L, H, Dv)

def first_inputs(seed: int = 0) -> dict:
    key = jax.random.key(seed)
    ks = jax.random.split(key, 16)
    f32 = jnp.float32

    def nrm(k, shape, s):
        return jax.random.normal(k, shape, f32) * s

    x = nrm(ks[0], (BATCH, SEQ, D_MODEL), 1.0)
    mix_norm_gain = 1.0 + nrm(ks[1], (DEPTH, D_MODEL), 0.05)
    w_in = nrm(ks[2], (DEPTH, D_MODEL, IN_COLS), D_MODEL ** -0.5)
    att_q_gain = 1.0 + nrm(ks[3], (DEPTH, ATT_HEAD_DIM), 0.05)
    att_k_gain = 1.0 + nrm(ks[4], (DEPTH, ATT_HEAD_DIM), 0.05)
    rel_bias = nrm(ks[5], (DEPTH, ATT_HEADS, N_REL), 0.2)
    att_out_gain = 1.0 + nrm(ks[6], (DEPTH, ATT_WIDTH), 0.05)
    dn_conv_w = nrm(ks[7], (DEPTH, CONV_K, 3 * DN_WIDTH), CONV_K ** -0.5)
    dn_a_log = jnp.log(jax.random.uniform(ks[8], (DEPTH, DN_HEADS), f32, 1.0, 16.0))
    dt = jnp.exp(jax.random.uniform(ks[9], (DEPTH, DN_HEADS), f32,
                                    float(np.log(1e-3)), float(np.log(1e-1))))
    dn_dt_bias = dt + jnp.log(-jnp.expm1(-dt))
    dn_out_gain = 1.0 + nrm(ks[10], (DEPTH, DN_HEAD_DIM), 0.05)
    w_out = nrm(ks[11], (DEPTH, D_MODEL, D_MODEL), D_MODEL ** -0.5)
    ffn_norm_gain = 1.0 + nrm(ks[12], (DEPTH, D_MODEL), 0.05)
    w_ff1 = nrm(ks[13], (DEPTH, D_MODEL, D_FF), D_MODEL ** -0.5)
    w_ff2 = nrm(ks[14], (DEPTH, D_FF, D_MODEL), D_FF ** -0.5)
    return {"x": x, "mix_norm_gain": mix_norm_gain, "w_in": w_in,
            "att_q_gain": att_q_gain, "att_k_gain": att_k_gain, "rel_bias": rel_bias,
            "att_out_gain": att_out_gain, "dn_conv_w": dn_conv_w, "dn_a_log": dn_a_log,
            "dn_dt_bias": dn_dt_bias, "dn_out_gain": dn_out_gain, "w_out": w_out,
            "ffn_norm_gain": ffn_norm_gain, "w_ff1": w_ff1, "w_ff2": w_ff2}

def first_block(x, mix_norm_gain, w_in, att_q_gain, att_k_gain, rel_bias, att_out_gain,
              dn_conv_w, dn_a_log, dn_dt_bias, dn_out_gain, w_out, ffn_norm_gain,
              w_ff1, w_ff2):
    B, L, _ = x.shape
    h = x
    for layer in range(DEPTH):
        u = rms_norm(h, mix_norm_gain[layer])
        proj = u @ w_in[layer]
        aq, ak, av, dqkv, dgate, da, db = jnp.split(proj, SPLITS, axis=-1)
        shp_a = (B, L, ATT_HEADS, ATT_HEAD_DIM)
        o_att = chunked_rel_attention(aq.reshape(shp_a), ak.reshape(shp_a), av.reshape(shp_a),
                                      att_q_gain[layer], att_k_gain[layer], rel_bias[layer])
        o_att = rms_norm(o_att, att_out_gain[layer])
        dqkv = causal_short_conv(dqkv, dn_conv_w[layer])
        dq, dk, dv = jnp.split(dqkv, 3, axis=-1)
        shp_d = (B, L, DN_HEADS, DN_HEAD_DIM)
        log_decay = -jnp.exp(dn_a_log[layer].astype(jnp.float32)) * jax.nn.softplus(
            da.astype(jnp.float32) + dn_dt_bias[layer].astype(jnp.float32))
        beta = jax.nn.sigmoid(db.astype(jnp.float32))
        o_dn = gated_delta_rule(dq.reshape(shp_d), dk.reshape(shp_d), dv.reshape(shp_d),
                                log_decay, beta)
        o_dn = rms_norm(o_dn, dn_out_gain[layer]) * jax.nn.silu(
            dgate.reshape(shp_d).astype(jnp.float32))
        o_dn = o_dn.reshape(B, L, DN_WIDTH).astype(h.dtype)
        mixed = jnp.concatenate([o_att, o_dn], axis=-1) @ w_out[layer]
        h = h + mixed
        z = rms_norm(h, ffn_norm_gain[layer]) @ w_ff1[layer]
        h = h + jnp.square(jax.nn.relu(z)) @ w_ff2[layer]
    return h


RET_HEADS = 4
RET_DK = 128
RET_DV = 256
RET_CHUNK = 128
DIFF_HEADS = 4
DIFF_DK = 128
DIFF_DV = 256
Q_BLOCK = 128
ROPE_THETA = 10000.0
N_GROUPS = 4
EXPERTS_PER_GROUP = 8
N_EXPERTS = 32
TOP_K = 2
D_EXPERT = 512
MOE_BLOCK = 128

RET_QK = 512
RET_V = 1024
DIFF_QK = 1024
DIFF_V = 1024
IN_OFFSETS = (512, 1024, 2048, 3072, 4096, 5120, 6144, 7168)
D_IN = 8192


def rmsnorm(x, g):
    xf = x.astype(jnp.float32)
    y = xf * lax.rsqrt(jnp.mean(xf * xf, axis=-1, keepdims=True) + EPS)
    return (y * g.astype(jnp.float32)).astype(x.dtype)

def head_rms(o):
    of = o.astype(jnp.float32)
    return of * lax.rsqrt(jnp.mean(of * of, axis=-1, keepdims=True) + EPS)

def apply_rope(t, positions):
    d = t.shape[-1]
    inv = ROPE_THETA ** (-jnp.arange(0, d, 2, dtype=jnp.float32) / d)
    ang = positions.astype(jnp.float32)[:, :, None] * inv
    cos = jnp.cos(ang)[:, :, None, :]
    sin = jnp.sin(ang)[:, :, None, :]
    tf = t.astype(jnp.float32)
    t1, t2 = tf[..., : d // 2], tf[..., d // 2:]
    return jnp.concatenate([t1 * cos - t2 * sin, t2 * cos + t1 * sin], axis=-1).astype(t.dtype)

def retention(q, k, v):
    B, S, H, dk = q.shape
    dv = v.shape[-1]
    C = RET_CHUNK
    N = S // C
    gamma = 1.0 - jnp.exp2(-5.0 - jnp.arange(H, dtype=jnp.float32))
    log_g = jnp.log(gamma)
    idx = jnp.arange(C, dtype=jnp.float32)
    rel = idx[:, None] - idx[None, :]
    dmask = jnp.where(rel >= 0, jnp.exp(log_g[:, None, None] * jnp.maximum(rel, 0.0)), 0.0)
    zeta = jnp.exp(log_g[:, None] * (C - 1 - idx)).T
    xi = jnp.exp(log_g[:, None] * (idx + 1)).T
    chunk_decay = jnp.exp(log_g * C)
    qc = q.astype(jnp.float32).reshape(B, N, C, H, dk)
    kc = k.astype(jnp.float32).reshape(B, N, C, H, dk) * (dk ** -0.5)
    vc = v.astype(jnp.float32).reshape(B, N, C, H, dv)
    s = jnp.einsum('bnihd,bnjhd->bnhij', qc, kc) * dmask
    o_in = jnp.einsum('bnhij,bnjhe->bnihe', s, vc)
    kv = jnp.einsum('bnjhd,bnjhe->bnhde', kc * zeta[None, None, :, :, None], vc)

    def step(state, kv_n):
        return chunk_decay[None, :, None, None] * state + kv_n, state

    _, state_prev = lax.scan(step, jnp.zeros((B, H, dk, dv), jnp.float32), jnp.swapaxes(kv, 0, 1))
    o_cross = jnp.einsum('bnihd,nbhde->bnihe', qc * xi[None, None, :, :, None], state_prev)
    return (o_in + o_cross).reshape(B, S, H, dv)

def diff_attention(q, k, v, lam):
    B, S, H, _, dk = q.shape
    dv = v.shape[-1]
    nq = S // Q_BLOCK
    qb = jnp.moveaxis(q.reshape(B, nq, Q_BLOCK, H, 2, dk), 1, 0)
    kpos = jnp.arange(S)
    scale = dk ** -0.5
    neg = jnp.finfo(jnp.float32).min

    def block(args):
        i, qi = args
        s = jnp.einsum('bqhcd,bkhcd->bhcqk', qi, k).astype(jnp.float32) * scale
        qpos = i * Q_BLOCK + jnp.arange(Q_BLOCK)
        s = jnp.where(kpos[None, :] <= qpos[:, None], s, neg)
        p = jax.nn.softmax(s, axis=-1)
        a = p[:, :, 0] - lam * p[:, :, 1]
        return jnp.einsum('bhqk,bkhe->bqhe', a.astype(v.dtype), v)

    o = lax.map(block, (jnp.arange(nq), qb))
    return jnp.moveaxis(o, 0, 1).reshape(B, S, H, dv)

def hierarchical_moe(h, w_rg, b_rg, w_re, b_re, w1, w3, w2):
    T, D = h.shape
    gp = jax.nn.softmax(jnp.dot(h, w_rg).astype(jnp.float32) + b_rg, axis=-1)
    g_top, g_idx = lax.top_k(gp, 1)
    el_all = (jnp.dot(h, w_re).astype(jnp.float32) + b_re).reshape(T, N_GROUPS, EXPERTS_PER_GROUP)
    el = jnp.take_along_axis(el_all, g_idx[:, :, None], axis=1)[:, 0]
    e_val, e_idx = lax.top_k(el, TOP_K)
    weights = (g_top * jax.nn.softmax(e_val, axis=-1)).astype(h.dtype)
    expert = g_idx * EXPERTS_PER_GROUP + e_idx

    flat_e = expert.reshape(-1)
    A = flat_e.shape[0]
    order = jnp.argsort(flat_e)
    sorted_e = flat_e[order]
    counts = jnp.bincount(flat_e, length=N_EXPERTS)
    starts = jnp.cumsum(counts) - counts
    padded = ((counts + MOE_BLOCK - 1) // MOE_BLOCK) * MOE_BLOCK
    pad_ends = jnp.cumsum(padded)
    pad_starts = pad_ends - padded
    dest = pad_starts[sorted_e] + (jnp.arange(A) - starts[sorted_e])
    n_blocks = -(-A // MOE_BLOCK) + N_EXPERTS
    P = n_blocks * MOE_BLOCK
    row_token = jnp.full((P,), T, jnp.int32).at[dest].set((order // TOP_K).astype(jnp.int32))
    block_e = jnp.minimum(jnp.searchsorted(pad_ends, jnp.arange(n_blocks) * MOE_BLOCK, side='right'),
                          N_EXPERTS - 1)
    h_pad = jnp.concatenate([h, jnp.zeros((1, D), h.dtype)], axis=0)[row_token]
    h_pad = h_pad.reshape(n_blocks, MOE_BLOCK, D)

    def expert_block(args):
        xb, e = args
        return jnp.dot(jax.nn.silu(jnp.dot(xb, w1[e])) * jnp.dot(xb, w3[e]), w2[e])

    y_pad = lax.map(expert_block, (h_pad, block_e)).reshape(P, D)
    dest_of_flat = jnp.zeros((A,), jnp.int32).at[order].set(dest.astype(jnp.int32))
    y_assign = y_pad[dest_of_flat].reshape(T, TOP_K, D)
    return jnp.sum(y_assign * weights[:, :, None], axis=1)

def second_inputs(seed: int = 0) -> dict:
    key = jax.random.key(seed)
    ks = jax.random.split(key, 24)
    f32 = jnp.float32
    D = D_MODEL

    def nrm(k, shape, scale):
        return jax.random.normal(k, shape, f32) * scale

    return {
        "x": nrm(ks[0], (BATCH, SEQ, D), 1.0),
        "c": nrm(ks[1], (BATCH, D), 1.0),
        "positions": jnp.broadcast_to(jnp.arange(SEQ, dtype=jnp.int32)[None, :], (BATCH, SEQ)),
        "w_ada": nrm(ks[2], (DEPTH, D, 6 * D), D ** -0.5),
        "b_ada": nrm(ks[3], (DEPTH, 6 * D), 0.02),
        "norm_mix": 1.0 + nrm(ks[4], (DEPTH, D), 0.02),
        "w_in": nrm(ks[5], (DEPTH, D, D_IN), D ** -0.5),
        "w_ret_o": nrm(ks[6], (DEPTH, RET_V, D), RET_V ** -0.5),
        "w_diff_o": nrm(ks[7], (DEPTH, DIFF_V, D), DIFF_V ** -0.5),
        "lam_q1": nrm(ks[8], (DEPTH, DIFF_DK), 0.1),
        "lam_k1": nrm(ks[9], (DEPTH, DIFF_DK), 0.1),
        "lam_q2": nrm(ks[10], (DEPTH, DIFF_DK), 0.1),
        "lam_k2": nrm(ks[11], (DEPTH, DIFF_DK), 0.1),
        "diff_norm": 1.0 + nrm(ks[12], (DEPTH, DIFF_DV), 0.02),
        "w_out": nrm(ks[13], (DEPTH, D, D), D ** -0.5),
        "norm_ffn": 1.0 + nrm(ks[14], (DEPTH, D), 0.02),
        "w_router_group": nrm(ks[15], (DEPTH, D, N_GROUPS), D ** -0.5),
        "b_router_group": nrm(ks[16], (DEPTH, N_GROUPS), 0.01),
        "w_router_expert": nrm(ks[17], (DEPTH, D, N_GROUPS * EXPERTS_PER_GROUP), D ** -0.5),
        "b_router_expert": nrm(ks[18], (DEPTH, N_GROUPS * EXPERTS_PER_GROUP), 0.01),
        "w_exp_gate": nrm(ks[19], (DEPTH, N_EXPERTS, D, D_EXPERT), D ** -0.5),
        "w_exp_up": nrm(ks[20], (DEPTH, N_EXPERTS, D, D_EXPERT), D ** -0.5),
        "w_exp_down": nrm(ks[21], (DEPTH, N_EXPERTS, D_EXPERT, D), D_EXPERT ** -0.5),
        "norm_final": 1.0 + nrm(ks[22], (D,), 0.02),
    }

def second_block(x, c, positions, w_ada, b_ada, norm_mix, w_in, w_ret_o, w_diff_o,
              lam_q1, lam_k1, lam_q2, lam_k2, diff_norm, w_out, norm_ffn,
              w_router_group, b_router_group, w_router_expert, b_router_expert,
              w_exp_gate, w_exp_up, w_exp_down, norm_final):
    B, S, D = x.shape
    for l in range(DEPTH):
        lambda_init = 0.8 - 0.6 * math.exp(-0.3 * l)
        mod = (jnp.dot(jax.nn.silu(c), w_ada[l]) + b_ada[l])[:, None, :]
        sh1, sc1, g1, sh2, sc2, g2 = jnp.split(mod, 6, axis=-1)

        h = rmsnorm(x, norm_mix[l]) * (1.0 + sc1) + sh1
        proj = jnp.dot(h, w_in[l])
        rq, rk, rv, rg, dq, dk, dv, gate_r, gate_d = jnp.split(proj, list(IN_OFFSETS), axis=-1)

        rq = apply_rope(rq.reshape(B, S, RET_HEADS, RET_DK), positions)
        rk = apply_rope(rk.reshape(B, S, RET_HEADS, RET_DK), positions)
        ro = retention(rq, rk, rv.reshape(B, S, RET_HEADS, RET_DV))
        ro = head_rms(ro).reshape(B, S, RET_V).astype(x.dtype) * jax.nn.silu(rg)
        ret_out = jnp.dot(ro, w_ret_o[l])

        dq = apply_rope(dq.reshape(B, S, 2 * DIFF_HEADS, DIFF_DK), positions).reshape(B, S, DIFF_HEADS, 2, DIFF_DK)
        dk = apply_rope(dk.reshape(B, S, 2 * DIFF_HEADS, DIFF_DK), positions).reshape(B, S, DIFF_HEADS, 2, DIFF_DK)
        lam = (jnp.exp(jnp.sum(lam_q1[l].astype(jnp.float32) * lam_k1[l].astype(jnp.float32)))
               - jnp.exp(jnp.sum(lam_q2[l].astype(jnp.float32) * lam_k2[l].astype(jnp.float32)))
               + lambda_init)
        do = diff_attention(dq, dk, dv.reshape(B, S, DIFF_HEADS, DIFF_DV), lam)
        do = head_rms(do) * diff_norm[l].astype(jnp.float32) * (1.0 - lambda_init)
        diff_out = jnp.dot(do.reshape(B, S, DIFF_V).astype(x.dtype), w_diff_o[l])

        merged = jax.nn.sigmoid(gate_r) * ret_out + jax.nn.sigmoid(gate_d) * diff_out
        x = x + g1 * jnp.dot(merged, w_out[l])

        h2 = rmsnorm(x, norm_ffn[l]) * (1.0 + sc2) + sh2
        y = hierarchical_moe(h2.reshape(B * S, D), w_router_group[l], b_router_group[l],
                             w_router_expert[l], b_router_expert[l],
                             w_exp_gate[l], w_exp_up[l], w_exp_down[l]).reshape(B, S, D)
        x = x + g2 * y
    return rmsnorm(x, norm_final)


def setup_inputs(seed=0):
    out = dict(first_inputs(seed))
    for name, value in second_inputs(seed + 1).items():
        if name != "x":
            out[name + "_2"] = value
    return out


def reference(
    x, mix_norm_gain, w_in, att_q_gain, att_k_gain, rel_bias, att_out_gain, dn_conv_w, dn_a_log,
    dn_dt_bias, dn_out_gain, w_out, ffn_norm_gain, w_ff1, w_ff2, c_2, positions_2, w_ada_2,
    b_ada_2, norm_mix_2, w_in_2, w_ret_o_2, w_diff_o_2, lam_q1_2, lam_k1_2, lam_q2_2, lam_k2_2,
    diff_norm_2, w_out_2, norm_ffn_2, w_router_group_2, b_router_group_2, w_router_expert_2,
    b_router_expert_2, w_exp_gate_2, w_exp_up_2, w_exp_down_2, norm_final_2,
):
    x = first_block(
        x, mix_norm_gain, w_in, att_q_gain, att_k_gain, rel_bias, att_out_gain, dn_conv_w,
        dn_a_log, dn_dt_bias, dn_out_gain, w_out, ffn_norm_gain, w_ff1, w_ff2,
    )
    return second_block(
        x, c_2, positions_2, w_ada_2, b_ada_2, norm_mix_2, w_in_2, w_ret_o_2, w_diff_o_2,
        lam_q1_2, lam_k1_2, lam_q2_2, lam_k2_2, diff_norm_2, w_out_2, norm_ffn_2,
        w_router_group_2, b_router_group_2, w_router_expert_2, b_router_expert_2, w_exp_gate_2,
        w_exp_up_2, w_exp_down_2, norm_final_2,
    )


_drawn_inputs = setup_inputs


def setup_inputs(seed=0):
    import zlib

    import numpy as np

    out = dict(_drawn_inputs(seed))
    spreads = {}
    factors = {'norm_mix_2': 4.327,
     'lam_k2_2': 7.211,
     'diff_norm_2': 8.0,
     'norm_ffn_2': 3.318,
     'b_router_group_2': 4.919,
     'b_router_expert_2': 6.381,
     'norm_final_2': 2.945}
    for name, (base, spread) in spreads.items():
        noise = np.random.default_rng([zlib.crc32(name.encode()), seed]).standard_normal(out[name].shape)
        drawn = base * np.exp(spread * noise) if base else spread * noise
        out[name] = __import__('jax').numpy.asarray(drawn.astype(out[name].dtype))
    for name, factor in factors.items():
        out[name] = (out[name] * factor).astype(out[name].dtype)
    return out
```

```python
import numpy as np
import concourse.bass as bass
from concourse import mybir
from contextlib import ExitStack

P = 128
T = 2
D = 1024
KT = D // P
WC = 512
SLOT = KT * WC
EPS = 1e-6
NEG = -1e30
AH, AD = 8, 64
NREL = 513
MAXREL = 256
DH, DD = 4, 128
C = 64
FF = 4096
RH, RK, RV = 4, 128, 256
E, EG, NG, DE = 32, 8, 4, 512
LEVELS = [2, 4, 8, 16, 32]
THETA = 10000.0
NROWS = 18
LAMI = 0.8 - 0.6


CONST = {}


def constants():
    i = np.arange(P)
    row, col = i[:, None], i[None, :]
    same = (row // C) == (col // C)
    parts = []

    def put(name, a):
        a = np.asarray(a, np.float32).reshape(P, -1)
        CONST[name] = (sum(x.shape[1] for x in parts), a.shape[1])
        parts.append(a)

    put("ident", np.eye(P))
    put("flip", np.eye(P)[::-1])
    put("ones", np.ones((P, P)))
    put("cumT", same & (row <= col))
    put("blk", same)
    put("negT", np.where(same & (row <= col), 0.0, NEG))
    for s in [1] + LEVELS:
        m = (col // (2 * s) == row // (2 * s)) & ((col // s) % 2 == 1) & ((row // s) % 2 == 0)
        put(f"lvl{s}", -1.0 * m)
    put("causT", np.where(row <= col, 0.0, NEG))
    gamma = 1.0 - np.exp2(-5.0 - np.arange(RH, dtype=np.float32))
    logg = np.log(gamma.astype(np.float32)).astype(np.float32)
    rel = (col - row).astype(np.float32)
    dm = np.stack([np.where(rel >= 0, np.exp(logg[h] * np.maximum(rel, 0)), 0.0) for h in range(RH)], 1)
    put("dmaskT", dm * RK ** -0.5)
    put("zeta", np.exp(logg[None, :] * (P - 1 - i[:, None])) * RK ** -0.5)
    put("xi", np.exp(logg[None, :] * (i[:, None] + 1)))
    inv = (np.float32(THETA) ** (-np.arange(0, RK, 2, dtype=np.float32) / RK)).astype(np.float32)
    put("half", np.stack([i < C, i >= C], 1))
    put("prio", np.broadcast_to(np.arange(E, 0, -1), (P, E)))
    put("inv", np.broadcast_to(inv, (P, RK // 2)))
    return np.ascontiguousarray(np.concatenate(parts, 1))


COLS = [("c", 8), ("mix", 8), ("attout", 4), ("dnout", 1), ("ffn", 8), ("nmix", 8), ("nffn", 8),
        ("dnorm", 2), ("bada", 48), ("qg", 1), ("kg", 1), ("lam", 4)]


def program(nc, g, out):
    fp32, i32 = mybir.dt.float32, mybir.dt.int32
    ALU, ACT, AX = mybir.AluOpType, mybir.ActivationFunctionType, mybir.AxisListType
    ctx = ExitStack()
    with ctx:
        def sb(name, n, dt=fp32):
            return ctx.enter_context(nc.sbuf_tensor(name, [P, n], dt))

        ncon = g["const"].shape[1]
        NR = 4
        ring = sb("ring", NR * SLOT)
        con = sb("con", ncon)
        X = sb("X", T * D)
        actT = sb("actT", KT * T * P)
        tok = sb("tok", T * D)
        rowsA = sb("rowsA", P)
        rowsB = sb("rowsB", P)
        colA = sb("colA", 104)
        colB = sb("colB", 48)
        small = sb("small", 464)
        posi = sb("posi", 2, i32)
        NA = 26980
        arena = sb("arena", NA)
        banks = [ctx.enter_context(nc.psum_tensor(f"bank{i}", [P, 512], fp32)) for i in range(8)]

        def K(name):
            o, n = CONST[name]
            return con[:, o:o + n]

        ident, ones, flip = K("ident"), K("ones"), K("flip")
        colat, o = {}, 0
        for name, n in COLS:
            colat[name] = o
            o += n
        NCOL = o

        def col(name, i=0, n=1):
            return colA[:, colat[name] + i:colat[name] + i + n]

        at = {"n": 0}

        def sm(n):
            at["n"] += n
            assert at["n"] <= 464
            return small[:, at["n"] - n:at["n"]]

        def ar(o, n):
            assert o + n <= NA, (o, n)
            return arena[:, o:o + n]

        X3 = X[:, :].rearrange("p (t d) -> p t d", t=T)
        tok3 = tok[:, :].rearrange("p (t d) -> p t d", t=T)
        aT = actT[:, :].rearrange("p (k n) -> p k n", k=KT)

        def slot(i):
            return ring[:, (i % NR) * SLOT:(i % NR + 1) * SLOT]

        av = ar(0, 1024)
        gate = ar(1024, 1024)
        oatt = ar(2048, 1024)
        odn = ar(3072, 1024)
        DQ, DK, DV = ar(4096, 1024), ar(5120, 1024), ar(6144, 1024)
        R0 = 7168
        CW = T * P + 3
        cin = ar(R0, 12 * CW).rearrange("p (f n) -> p f n", f=12)
        cout = ar(R0 + 3200, 3072).rearrange("p (f n) -> p f n", f=12)
        cexp = ar(R0 + 6400, 1024)
        qktok = ar(R0 + 7424, 2048)
        asq = ar(R0 + 9472, 2048)
        aqkT = ar(R0 + 11520, 2048)
        bias = ar(R0 + 13568, 3072).rearrange("p (h n) -> p h n", h=AH)
        aP = ar(R0, 3072).rearrange("p (h n) -> p h n", h=AH)
        aPT = ar(R0 + 3200, 3072).rearrange("p (h n) -> p h n", h=AH)
        gexp = ar(R0 + 6400, 1024)
        KB, KBE, KTL, QD = [ar(R0 + 1024 * i, 1024) for i in range(4)]
        kT, kbT, qT, qdT = [ar(R0 + 4096 + 1024 * i, 1024) for i in range(4)]
        ET, AT, MT, DI, DT, YY, AM, VAL, KC, VN = [ar(R0 + 8192 + 1024 * i, 1024) for i in range(10)]
        ST = ar(R0 + 18432, 512)
        dsq = AM
        zT = ar(0, 8192).rearrange("p (f n) -> p f n", f=32)
        zr = ar(8192, 1024)
        qkT2 = ar(0, 6144).rearrange("p (c h n) -> p c h n", c=6, h=RH)
        RVt, DVt, RG, GR, GD = [ar(6144 + 2048 * i, 2048) for i in range(5)]
        ropeA, ropeB = ar(16384, 512), ar(16896, 512)
        ropeO = ar(17408, 1024)
        KZ = ar(18432, 512)
        sT = ar(18944, 1024)
        KV = ar(19968, 1024)
        P2 = ar(20992, 3072).rearrange("p (h n) -> p h n", h=8)
        PT2 = ar(24064, 1536).rearrange("p (h n) -> p h n", h=4)
        gex = ar(25600, 1024)
        grow1, grow2 = ar(6144, 1024), ar(7168, 1024)
        gdiag = ar(0, 2048)
        sq2 = ar(16384, 2048)
        Y = ar(0, 2048).rearrange("p (t d) -> p t d", t=T)
        hid = ar(2048, 1024)
        hex_ = ar(3072, 1024)
        wr = ar(4096, 8 * 36).rearrange("p (k n) -> p k n", k=KT)
        G2 = ar(7168, 1024)
        fing = ar(8192, 1024)
        XS = 12288
        xslots = [ar(XS, SLOT), ar(XS + SLOT, SLOT)]

        ss = sm(2); lnv = sm(16); rstd = sm(2)
        a_ss = sm(32); a_rs = sm(32); a_mx = sm(16); a_sum = sm(16); a_rd = sm(16)
        n_ss = sm(16); n_rs = sm(16)
        dtb = sm(4); alog = sm(4); ea = sm(4)
        dadb = sm(16); t1 = sm(8); t2 = sm(8); t3 = sm(8); gl = sm(8); beta = sm(8); dnt = sm(8)
        dec = sm(32); ghalf = sm(16); edec = sm(8); etl = sm(8); ecd = sm(16)
        cs = sm(8); cex = sm(8)
        modc = sm(48); sc1 = sm(8); sc2 = sm(8)
        EPSC = sm(1)
        posf = sm(2); dng = sm(2); qg8 = sm(1)
        lamp = sm(2); lame = sm(2); lam = sm(1)
        rbias = sm(36)
        angle, angk = ar(3072, 256), ar(3328, 256)
        cosin = sb("cosin", 4 * 64)
        lg, rt, rt2, rt3, rs8, Wt = [ar(4400 + 72 * i, 72) for i in range(6)]
        Wt = Wt[:, 0:64]

        names = """x_in rows_in const_in vec_in bias_in pos_in wr_in fin_in ada_used ff2_used
                 dve_step act_step pool_step n1_rs n1_tok n2_rs n2_tok n3_rs n3_tok n4_rs n4_tok n5_rs
                 cin_zero eps_set gate2 y_done conv_y conv_e conv_done dn_ss dn_rs a_ss a_rs a_qn a_max a_exp bias_masked gexp_done
                 c_exp c_silu ang_ready ang_done gl_req gl_exp g_ready cumg dec_ready dec_exp et_req et_exp
                 dscaled at_ready d_init am_ready vn_new s_new odn_ready gate_done o_ss o_rs o_tok x1_new
                 z_relu z_done x2_new rope_out kz_done st_done g_exp head_ss head_rs r_tok p_max p_exp a_done
                 lam_prod lam_exp m_done diag x3_new router_req router_exp w_moe e_exp e_free hid_done y_zero
                 wr_free fin_free out_done store mo_step ma_step""".split()
        S = {n: ctx.enter_context(nc.semaphore(n)) for n in names}
        w_in = [ctx.enter_context(nc.semaphore(f"w_in{i}")) for i in range(NR)]
        wx_in = [ctx.enter_context(nc.semaphore(f"wx_in{i}")) for i in range(2)]
        full = [ctx.enter_context(nc.semaphore(f"bank_full{i}")) for i in range(8)]
        read = [ctx.enter_context(nc.semaphore(f"bank_read{i}")) for i in range(8)]

        order = ([("win", c) for c in (3, 4, 5, 7, 0, 1, 2, 6)] + [("ada", c) for c in range(12)]
                 + [("wout", c) for c in range(2)]
                 + [("ff1", c) for c in range(8)] + [("ff2", c) for c in range(8)]
                 + [("win2", c) for c in range(16)]
                 + [("wret", c) for c in range(2)] + [("wdiff", c) for c in range(2)]
                 + [("wout2", c) for c in range(2)])
        NW = len(order)
        place = {k: n for n, k in enumerate(order)}
        assert NW % NR == 0
        wsrc = {"win": g["w_in"], "ada": g["w_ada_2"], "wout": g["w_out"], "ff1": g["w_ff1"], "ff2": g["w_ff2"],
                "win2": g["w_in_2"], "wret": g["w_ret_o_2"], "wdiff": g["w_diff_o_2"], "wout2": g["w_out_2"]}

        def weights(kind, c):
            s = slot(place[(kind, c)])
            return s.rearrange("p (k n) -> p k n", k=4 if kind == "ff2" else KT)

        def mslot(s):
            return slot(s) if s < NR else xslots[s - NR]

        def moe_in(s, it):
            return (w_in[s], 16 * (NW // NR + 1) + 16 * it) if s < NR else (wx_in[s - NR], 16 + 16 * it)

        last_job = {}

        uses, where, base = [0] * 8, {}, [0] * 8

        def job(name):
            b = sum(uses) % 8
            uses[b] += 1
            where[name] = (b, uses[b])
            return where[name]

        def wait_full(eng, name):
            b, u = where[name]
            eng.wait_ge(full[b], u)
            return banks[b]

        def wait_read(eng, name):
            b, u = where[name]
            eng.wait_ge(read[b], u)

        def done(ins, name):
            ins.then_inc(read[where[name][0]], 1)

        def bc(ap, n):
            return ap.unsqueeze(2).to_broadcast([P, ap.shape[1], n])

        def bm(ap, k):
            return ap.unsqueeze(1).to_broadcast([P, k, ap.shape[1]])

        def v3(ap, k):
            return ap.rearrange("p (k n) -> p k n", k=k)

        block = ctx.enter_context(nc.Block())

        @block.tensor
        def _(pe):
            mm = nc.tensor.matmul

            def begin(name):
                b, u = job(name)
                if u > 1:
                    pe.wait_ge(read[b], u - 1)
                return banks[b]

            def end(ins, name):
                ins.then_inc(full[where[name][0]], 1)

            def need(kind, c):
                n = place[(kind, c)]
                pe.wait_ge(w_in[n % NR], 16 * (n // NR + 1))
                return weights(kind, c)

            def transposes(name, src):
                for j in range(4):
                    bk = begin(f"{name}{j}")
                    for k in range(2):
                        for t in range(T):
                            i = nc.tensor.transpose(bk[:, (2 * k + t) * P:(2 * k + t + 1) * P],
                                                    src[:, t, (2 * j + k) * P:(2 * j + k + 1) * P], ident)
                    end(i, f"{name}{j}")

            def wait_actT(name):
                for j in range(4):
                    wait_read(pe, f"{name}{j}")

            def tok_product(kind, c, name, cols=WC):
                w = need(kind, c)
                for t in range(T):
                    bk = begin(f"{name}{t}")
                    for k in range(KT):
                        i = mm(bk[:, 0:cols], aT[:, k, t * P:(t + 1) * P], w[:, k, 0:cols], start=(k == 0), stop=(k == KT - 1))
                    end(i, f"{name}{t}")
                last_job[place[(kind, c)]] = f"{name}1"

            pe.wait_ge(S["rows_in"], 16 * NROWS)
            pe.wait_ge(S["const_in"], 16)
            bk = begin("cols")
            nc.tensor.transpose(bk[:, 0:NCOL], rowsA[0:NCOL, :], ident[0:NCOL, 0:NCOL])
            end(nc.tensor.transpose(bk[:, P:P + 48], rowsB[0:48, :], ident[0:48, 0:48]), "cols")
            pe.wait_ge(S["n1_tok"], 2)
            transposes("n1T", tok3)
            wait_actT("n1T")
            pe.wait_ge(S["lam_prod"], 1)
            bk = begin("lam")
            end(mm(bk[:, 0:2], ones, lamp, start=True, stop=True), "lam")
            for c in (3, 4, 5):
                w = need("win", c)
                for hh in range(2):
                    n = f"dp{c - 3}_{hh}"
                    bk = begin(n)
                    for f in range(2):
                        for k in range(KT):
                            i = mm(bk[:, f * 256:(f + 1) * 256], w[:, k, (2 * hh + f) * P:(2 * hh + f + 1) * P],
                                   aT[:, k, :], start=(k == 0), stop=(k == KT - 1))
                    end(i, n)
                last_job[place[("win", c)]] = n
            w = need("win", 7)
            bk = begin("dadb")
            for t in range(T):
                for k in range(KT):
                    i = mm(bk[:, t * 8:t * 8 + 8], aT[:, k, t * P:(t + 1) * P], w[:, k, 0:8],
                           start=(k == 0), stop=(k == KT - 1))
            end(i, "dadb")
            last_job[place[("win", 7)]] = "dadb"
            for c, n in ((0, "aq"), (1, "ak"), (2, "av"), (6, "dg")):
                tok_product("win", c, n)
            for x in range(3):
                pe.wait_ge(S["conv_done"], x + 1)
                for t in range(T):
                    n = f"ct{x}{t}"
                    bk = begin(n)
                    for h in range(DH):
                        i = nc.tensor.transpose(bk[:, h * P:(h + 1) * P], cout[:, 4 * x + h, t * P:(t + 1) * P], ident)
                    end(i, n)
            for x in range(2):
                for t in range(T):
                    pe.wait_ge(S["a_qn"], 2 * x + t + 1)
                    n = f"aT{x}{t}"
                    bk = begin(n)
                    for pr in range(4):
                        i = nc.tensor.transpose(bk[:, pr * P:(pr + 1) * P],
                                                v3(qktok, 4)[:, 2 * x + t, pr * P:(pr + 1) * P], ident)
                    end(i, n)
            pe.wait_ge(S["c_silu"], 1)
            bkm = begin("mod")
            for c in range(12):
                w = need("ada", c)
                for f in range(4):
                    for k in range(KT):
                        i = mm(bkm[:, 4 * c + f:4 * c + f + 1], w[:, k, f * P:(f + 1) * P], cs[:, k:k + 1],
                               start=(k == 0), stop=(k == KT - 1))
                if c < 11:
                    i.then_inc(S["ada_used"], 1)
            end(i, "mod")
            last_job[place[("ada", 11)]] = "mod"
            for x in range(2):
                for t in range(T):
                    wait_read(pe, f"aT{x}{t}")
            pe.wait_ge(S["bias_masked"], 1)
            qk4 = aqkT.rearrange("p (x r n) -> p x r n", x=2, r=4)
            for h in range(AH):
                pb, pr = 64 * (h % 2), h // 2
                bk = begin(f"as{h}")
                mm(bk[:, 0:P], qk4[pb:pb + 64, 0, pr, 0:P], qk4[pb:pb + 64, 1, pr, 0:P], start=True, stop=False)
                mm(bk[:, 0:P], bias[:, h, 0:P], flip, start=False, stop=True)
                mm(bk[:, P:384], qk4[pb:pb + 64, 0, pr, P:256], qk4[pb:pb + 64, 1, pr, 0:256], start=True, stop=False)
                mm(bk[:, P:256], bias[:, h, P:256], flip, start=False, stop=False)
                end(mm(bk[:, 256:384], bias[:, h, 256:384], flip, start=False, stop=True), f"as{h}")
            for h in range(AH):
                pe.wait_ge(S["a_exp"], h + 1)
                bk = begin(f"apT{h}")
                for j in range(3):
                    i = nc.tensor.transpose(bk[:, j * P:(j + 1) * P], aP[:, h, j * P:(j + 1) * P], ident)
                end(i, f"apT{h}")
            for h in range(AH):
                wait_read(pe, f"apT{h}")
            av3 = v3(av, 2)
            wait_read(pe, "av0")
            wait_read(pe, "av1")
            for t in range(T):
                bk = begin(f"ao{t}")
                for h in range(AH):
                    for j in range(t + 1):
                        i = mm(bk[:, h * AD:(h + 1) * AD], aPT[:, h, (t + j) * P:(t + j + 1) * P],
                               av3[:, j, h * AD:(h + 1) * AD], start=(j == 0), stop=(j == t))
                end(i, f"ao{t}")
            pe.wait_ge(S["g_ready"], 1)
            bk = begin("dec")
            mm(bk[:, 0:8], K("cumT"), gl, start=True, stop=True)
            mm(bk[:, 8:16], K("blk"), gl, start=True, stop=True)
            end(mm(bk[:, 16:32], ones, ghalf, start=True, stop=True), "dec")
            pe.wait_ge(S["cumg"], 1)
            for t in range(T):
                bk = begin(f"R{t}")
                end(mm(bk[:, :], ones, YY[:, t * 512:(t + 1) * 512], start=True, stop=True), f"R{t}")
            for x, src in enumerate((DK, KB, DQ, QD)):
                pe.wait_ge(S["dscaled"], x + 1)
                for t in range(T):
                    bk = begin(f"dT{x}{t}")
                    for h in range(DH):
                        o = (4 * t + h) * P
                        i = nc.tensor.transpose(bk[:, h * P:(h + 1) * P], src[:, o:o + P], ident)
                    end(i, f"dT{x}{t}")
            for x in range(3):
                for t in range(T):
                    wait_read(pe, f"dT{x}{t}")
            for x, rhs in enumerate((kbT, qT)):
                for t in range(T):
                    bk = begin(f"kk{x}{t}")
                    for h in range(DH):
                        o = (4 * t + h) * P
                        i = mm(bk[:, h * P:(h + 1) * P], kT[:, o:o + P], rhs[:, o:o + P], start=True, stop=True)
                    end(i, f"kk{x}{t}")
            for t in range(T):
                pe.wait_ge(S["d_init"], t + 1)
                bk = begin(f"D0{t}")
                for h in range(DH):
                    o = (4 * t + h) * P
                    i = nc.tensor.transpose(bk[:, h * P:(h + 1) * P], DT[:, o:o + P], ident)
                end(i, f"D0{t}")
            for l, s in enumerate(LEVELS):
                last = s == LEVELS[-1]
                for t in range(T):
                    pe.wait_ge(S["am_ready"], 2 * l + t + 1)
                    wait_read(pe, f"D0{t}" if l == 0 else f"Dn{l - 1}{t}")
                    bk = begin(f"Y{l}{t}")
                    for h in range(DH):
                        o = (4 * t + h) * P
                        i = mm(bk[:, h * P:(h + 1) * P], AM[:, o:o + P], DI[:, o:o + P], start=True, stop=True)
                    end(i, f"Y{l}{t}")
                for t in range(T):
                    wait_read(pe, f"Y{l}{t}")
                    if not last:
                        bk = begin(f"Dn{l}{t}")
                        for h in range(DH):
                            o = (4 * t + h) * P
                            i = mm(bk[:, h * P:(h + 1) * P], DT[:, o:o + P], YY[:, o:o + P], start=True, stop=True)
                        end(i, f"Dn{l}{t}")
                    bk = begin(f"Dt{l}{t}")
                    for h in range(DH):
                        o = (4 * t + h) * P
                        i = mm(bk[:, h * P:(h + 1) * P], YY[:, o:o + P], DT[:, o:o + P], start=True, stop=True)
                    end(i, f"Dt{l}{t}")
                for t in range(T):
                    wait_read(pe, f"Dt{l}{t}")
            for t in range(T):
                bk = begin(f"val{t}")
                for h in range(DH):
                    o = (4 * t + h) * P
                    i = mm(bk[:, h * P:(h + 1) * P], DT[:, o:o + P], DV[:, o:o + P], start=True, stop=True)
                end(i, f"val{t}")
                bk = begin(f"kc{t}")
                for h in range(DH):
                    o = (4 * t + h) * P
                    i = mm(bk[:, h * P:(h + 1) * P], KBE[:, o:o + P], DT[:, o:o + P], start=True, stop=True)
                end(i, f"kc{t}")
            for n in range(4):
                t, r = n // 2, C * (n % 2)
                if n == 0:
                    for x in (0, 1):
                        wait_read(pe, f"kc{x}")
                        wait_read(pe, f"dT3{x}")
                else:
                    pe.wait_ge(S["s_new"], n)
                    bk = begin(f"vp{n}")
                    for h in range(DH):
                        o = (4 * t + h) * P
                        i = mm(bk[r:r + C, h * P:(h + 1) * P], KC[:, o + r:o + r + C], ST[:, h * P:(h + 1) * P],
                               start=True, stop=True)
                    end(i, f"vp{n}")
                pe.wait_ge(S["vn_new"], n + 1)
                if n < 3:
                    bk = begin(f"sn{n}")
                    for h in range(DH):
                        o = (4 * t + h) * P
                        i = mm(bk[:, h * P:(h + 1) * P], KTL[r:r + C, o:o + P], VN[r:r + C, o:o + P],
                               start=True, stop=True)
                    end(i, f"sn{n}")
                bk = begin(f"do{n}")
                for h in range(DH):
                    o = (4 * t + h) * P
                    if n:
                        mm(bk[r:r + C, h * P:(h + 1) * P], qdT[:, o + r:o + r + C], ST[:, h * P:(h + 1) * P],
                           start=True, stop=False)
                    i = mm(bk[r:r + C, h * P:(h + 1) * P], MT[r:r + C, o + r:o + r + C], VN[r:r + C, o:o + P],
                           start=(n == 0), stop=True)
                end(i, f"do{n}")
            pe.wait_ge(S["o_tok"], 1)
            transposes("oT", tok3)
            wait_actT("oT")
            for c in range(2):
                tok_product("wout", c, f"mo{c}")
            pe.wait_ge(S["n2_tok"], 2)
            transposes("n2T", tok3)
            wait_actT("n2T")
            for c in range(8):
                w = need("ff1", c)
                for hh in range(2):
                    n = f"z{2 * c + hh}"
                    bk = begin(n)
                    for f in range(2):
                        for k in range(KT):
                            i = mm(bk[:, f * 256:(f + 1) * 256], w[:, k, (2 * hh + f) * P:(2 * hh + f + 1) * P],
                                   aT[:, k, :], start=(k == 0), stop=(k == KT - 1))
                    end(i, n)
                last_job[place[("ff1", c)]] = n
            bks = [begin(f"y{j}") for j in range(4)]
            for c in range(8):
                w = need("ff2", c)
                pe.wait_ge(S["z_done"], 2 * c + 2)
                for f in range(4):
                    for j in range(4):
                        t, hh = j // 2, j % 2
                        i = mm(bks[j][:, :], zT[:, 4 * c + f, t * P:(t + 1) * P], w[:, f, hh * 512:(hh + 1) * 512],
                               start=(c == 0 and f == 0), stop=(c == 7 and f == 3))
                        if c == 7 and f == 3 and j < 3:
                            end(i, f"y{j}")
                if c < 7:
                    i.then_inc(S["ff2_used"], 1)
                else:
                    end(i, "y3")
                    last_job[place[("ff2", 7)]] = "y3"
            pe.wait_ge(S["n3_tok"], 2)
            transposes("n3T", tok3)
            wait_actT("n3T")
            ROPE = {0: 0, 1: 1, 6: 2, 7: 3, 8: 4, 9: 5}

            def rope_transposes(x):
                for t in range(T):
                    pe.wait_ge(S["rope_out"], 2 * x + t + 1)
                    n = f"rT{x}{t}"
                    bk = begin(n)
                    for h in range(RH):
                        i = nc.tensor.transpose(bk[:, h * P:(h + 1) * P],
                                                ropeO[:, t * 512 + h * P:t * 512 + (h + 1) * P], ident)
                    end(i, n)

            pend = []
            for c in range(16):
                tok_product("win2", c, f"p{c}_")
                for x in pend:
                    rope_transposes(x)
                pend = [ROPE[c]] if c in ROPE else []
            for x in range(6):
                for t in range(T):
                    wait_read(pe, f"rT{x}{t}")
            for t in range(T):
                bk = begin(f"rs{t}")
                for h in range(RH):
                    i = mm(bk[:, h * P:(h + 1) * P], qkT2[:, 1, h, t * P:(t + 1) * P], qkT2[:, 0, h, t * P:(t + 1) * P],
                           start=True, stop=True)
                end(i, f"rs{t}")
            pe.wait_ge(S["kz_done"], 1)
            for c in (2, 3):
                for t in range(T):
                    wait_read(pe, f"p{c}_{t}")
            for hh in range(2):
                bk = begin(f"kv{hh}")
                for h in range(2):
                    hd = 2 * hh + h
                    i = mm(bk[:, h * 256:(h + 1) * 256], KZ[:, hd * P:(hd + 1) * P], RVt[:, hd * 256:(hd + 1) * 256],
                           start=True, stop=True)
                end(i, f"kv{hh}")
            for t in range(T):
                pe.wait_ge(S["st_done"], t + 1)
                for hh in range(2):
                    bk = begin(f"ro{t}{hh}")
                    for h in range(2):
                        hd = 2 * hh + h
                        i = mm(bk[:, h * 256:(h + 1) * 256], sT[:, t * 512 + hd * P:t * 512 + (hd + 1) * P],
                               RVt[:, t * 1024 + hd * 256:t * 1024 + (hd + 1) * 256], start=True, stop=True)
                    end(i, f"ro{t}{hh}")
            for hh in range(2):
                wait_read(pe, f"kv{hh}")
                bk = begin(f"rx{hh}")
                for h in range(2):
                    hd = 2 * hh + h
                    i = mm(bk[:, h * 256:(h + 1) * 256], qkT2[:, 0, hd, P:256], KV[:, hd * 256:(hd + 1) * 256],
                           start=True, stop=True)
                end(i, f"rx{hh}")
            for x in range(8):
                h, cc = x // 2, x % 2
                hq = 2 * h + cc
                q = qkT2[:, 2 + hq // 4, hq % 4, :]
                k = qkT2[:, 4 + hq // 4, hq % 4, :]
                bk = begin(f"ps{x}")
                mm(bk[:, 0:P], q[:, 0:P], k[:, 0:P], start=True, stop=False)
                mm(bk[:, 0:P], K("causT"), ident, start=False, stop=True)
                mm(bk[:, P:384], q[:, P:256], k[:, 0:256], start=True, stop=False)
                end(mm(bk[:, 256:384], K("causT"), ident, start=False, stop=True), f"ps{x}")
            pe.wait_ge(S["r_tok"], 2)
            transposes("rtT", tok3)
            wait_actT("rtT")
            for c in range(2):
                tok_product("wret", c, f"rp{c}")
            for h in range(RH):
                pe.wait_ge(S["a_done"], h + 1)
                bk = begin(f"pT{h}")
                for j in range(3):
                    i = nc.tensor.transpose(bk[:, j * P:(j + 1) * P], P2[:, 2 * h, j * P:(j + 1) * P], ident)
                end(i, f"pT{h}")
            for h in range(RH):
                wait_read(pe, f"pT{h}")
            for c in (10, 11):
                for t in range(T):
                    wait_read(pe, f"p{c}_{t}")
            for t in range(T):
                for hh in range(2):
                    bk = begin(f"po{t}{hh}")
                    for h in range(2):
                        hd = 2 * hh + h
                        for j in range(t + 1):
                            i = mm(bk[:, h * 256:(h + 1) * 256], PT2[:, hd, (t + j) * P:(t + j + 1) * P],
                                   DVt[:, j * 1024 + hd * 256:j * 1024 + (hd + 1) * 256], start=(j == 0), stop=(j == t))
                    end(i, f"po{t}{hh}")
            pe.wait_ge(S["r_tok"], 4)
            transposes("dtT", tok3)
            wait_actT("dtT")
            for c in range(2):
                tok_product("wdiff", c, f"wd{c}")
            pe.wait_ge(S["diag"], 1)
            for x in range(4):
                bk = begin(f"gr{x}")
                end(mm(bk[:, :], ones, gdiag[:, x * 512:(x + 1) * 512], start=True, stop=True), f"gr{x}")
            pe.wait_ge(S["m_done"], 1)
            transposes("mT", v3(GR, 2))
            wait_actT("mT")
            for c in range(2):
                tok_product("wout2", c, f"xo{c}")
            pe.wait_ge(S["n4_tok"], 2)
            transposes("n4T", tok3)
            wait_actT("n4T")
            pe.wait_ge(S["wr_in"], 32)
            bk = begin("rout")
            for t in range(T):
                for k in range(KT):
                    i = mm(bk[:, t * 36:t * 36 + 36], aT[:, k, t * P:(t + 1) * P], wr[:, k, :],
                           start=(k == 0), stop=(k == KT - 1))
            end(i, "rout")
            base[:] = uses
            for b in range(8):
                pe.wait_ge(read[b], base[b])
            with pe.Fori(0, E // 2) as it:
                for u in range(2):
                    for m in range(2):
                        s = 3 * u + m
                        pe.wait_ge(*moe_in(s, it))
                        w = v3(mslot(s), KT)
                        for hh in range(2):
                            b = 2 * m + hh
                            pe.wait_ge(read[b], base[b] + 2 * it + u)
                            for f in range(2):
                                for k in range(KT):
                                    i = mm(banks[b][:, f * 256:(f + 1) * 256],
                                           w[:, k, (2 * hh + f) * P:(2 * hh + f + 1) * P], aT[:, k, :],
                                           start=(k == 0), stop=(k == KT - 1))
                            i.then_inc(full[b], 1)
                    s = 3 * u + 2
                    pe.wait_ge(*moe_in(s, it))
                    w = v3(mslot(s), 4)
                    pe.wait_ge(S["hid_done"], 2 * it + u + 2)
                    for j in range(4):
                        t, hh = j // 2, j % 2
                        b = 4 + j
                        pe.wait_ge(read[b], base[b] + 2 * it + u)
                        for f in range(4):
                            i = mm(banks[b][:, :], hid[:, f * 256 + t * P:f * 256 + (t + 1) * P],
                                   w[:, f, hh * 512:(hh + 1) * 512], start=(f == 0), stop=(f == 3))
                        i.then_inc(full[b], 1)

        steps = {"dve_step": 0, "act_step": 0, "pool_step": 0}

        def chain(eng, ins, name):
            steps[name] += 1
            ins.then_inc(S[name], 1)
            eng.wait_ge(S[name], steps[name])

        GAIN = {"n1T": lambda k: (col("mix", k), None),
                "oT": lambda k: (col("attout", k) if k < 4 else col("dnout"), None),
                "n2T": lambda k: (col("ffn", k), None),
                "n3T": lambda k: (sc1[:, k:k + 1], modc[:, k:k + 1]),
                "rtT": lambda k: (None, None),
                "dtT": lambda k: (dng[:, k % 2:k % 2 + 1], None),
                "mT": lambda k: (None, None),
                "n4T": lambda k: (sc2[:, k:k + 1], modc[:, 24 + k:25 + k])}

        @block.scalar
        def _(act):
            A = nc.scalar.activation

            def step(ins):
                chain(act, ins, "act_step")

            def copy(o, i):
                return A(o, i, ACT.Copy)

            def rows(name, src, i=0):
                r = colat[name] + i
                act.dma_start(rowsA[r:r + src.shape[0], 0:src.shape[1]], src).then_inc(S["rows_in"], 16)

            act.dma_start(con[:, :], g["const"]).then_inc(S["const_in"], 16)
            for t in range(T):
                act.dma_start(X3[:, t, :], g["x"][0, t * P:(t + 1) * P, :]).then_inc(S["x_in"], 16)
            for name, key in (("c", "c_2"), ("mix", "mix_norm_gain"), ("attout", "att_out_gain"),
                              ("dnout", "dn_out_gain"), ("ffn", "ffn_norm_gain"), ("nmix", "norm_mix_2"),
                              ("nffn", "norm_ffn_2"), ("dnorm", "diff_norm_2"), ("bada", "b_ada_2")):
                rows(name, g[key].rearrange("o (k p) -> (o k) p", p=P))
            for name, key in (("qg", "att_q_gain"), ("kg", "att_k_gain")):
                for hh in range(2):
                    r = colat[name]
                    act.dma_start(rowsA[r:r + 1, hh * AD:(hh + 1) * AD], g[key]).then_inc(S["rows_in"], 16)
            for i, key in enumerate(("lam_q1_2", "lam_k1_2", "lam_q2_2", "lam_k2_2")):
                rows("lam", g[key], i)
            act.dma_start(rowsB[0:48, :], g["dn_conv_w"].rearrange("o j (f p) -> (o j f) p", p=P)).then_inc(S["rows_in"], 16)

            def inv_rms(o, i, n, width):
                step(A(lnv[:, 0:n], i, ACT.Ln, scale=1.0 / width, bias=EPSC))
                return A(o, lnv[:, 0:n], ACT.Exp, scale=-0.5)

            def norm(name):
                for t in range(T):
                    step(A(tok3[:, t, :], X3[:, t, :], ACT.Square, accum_out=ss[:, t:t + 1]))
                inv_rms(rstd, ss, T, D).then_inc(S[f"{name}_rs"], 1)

            def evac_T(name):
                for j in (0, 2):
                    bk = wait_full(act, f"{name}{j}")
                    for k in range(2):
                        sc, bi = GAIN[name](2 * j + k)
                        o = aT[:, 2 * j + k, :]
                        p = bk[:, k * 256:(k + 1) * 256]
                        if sc is None:
                            i = copy(o, p)
                        elif bi is None:
                            i = A(o, p, ACT.Copy, scale=sc)
                        else:
                            i = A(o, p, ACT.Identity, scale=sc, bias=bi)
                    done(i, f"{name}{j}")

            act.wait_ge(S["x_in"], 32)
            act.wait_ge(S["eps_set"], 1)
            norm("n1")
            act.wait_ge(S["ang_ready"], 1)
            A(cosin[:, :], angle[:, :], ACT.Sin).then_inc(S["ang_done"], 1)
            bk = wait_full(act, "cols")
            copy(colA[:, 0:NCOL], bk[:, 0:NCOL])
            done(copy(colB[:, :], bk[:, P:P + 48]), "cols")
            act.wait_ge(S["vec_in"], 64)
            wait_read(act, "cols")
            step(A(ea, alog, ACT.Exp))
            A(cex, col("c", 0, 8), ACT.Exp, scale=-1.0).then_inc(S["c_exp"], 1)
            evac_T("n1T")
            bk = wait_full(act, "lam")
            done(A(lame, bk[:, 0:2], ACT.Exp), "lam")
            for x in range(3):
                for hh in range(2):
                    n = f"dp{x}_{hh}"
                    bk = wait_full(act, n)
                    done(copy(cin[:, 4 * x + 2 * hh:4 * x + 2 * hh + 2, 3:CW], v3(bk[:, :], 2)), n)
                act.wait_ge(S["conv_y"], x + 1)
                A(cexp, cout[:, 4 * x:4 * x + 4, :], ACT.Exp, scale=-1.0).then_inc(S["conv_e"], 1)
            act.wait_ge(S["gl_req"], 1)
            step(A(t3, t2, ACT.Exp, scale=-1.0))
            step(A(t3, t3, ACT.Ln, bias=ones[:, 0:1]))
            A(v3(beta, 2), v3(dadb, 2)[:, :, 4:8], ACT.Exp, scale=-1.0).then_inc(S["gl_exp"], 1)
            for x, n in enumerate(("aq", "ak")):
                for t in range(T):
                    bk = wait_full(act, f"{n}{t}")
                    done(copy(v3(qktok, 4)[:, 2 * x + t, :], bk[:, :]), f"{n}{t}")
            for t in range(T):
                bk = wait_full(act, f"av{t}")
                done(copy(av[:, t * 512:(t + 1) * 512], bk[:, :]), f"av{t}")
            act.wait_ge(S["a_ss"], 4)
            step(A(a_rs, a_ss, ACT.Ln, scale=1.0 / AD, bias=EPSC))
            A(a_rs, a_rs, ACT.Exp, scale=-0.5).then_inc(S["a_rs"], 1)
            for t in range(T):
                bk = wait_full(act, f"dg{t}")
                step(copy(gate[:, t * 512:(t + 1) * 512], bk[:, :]))
                done(A(gexp[:, t * 512:(t + 1) * 512], bk[:, :], ACT.Exp, scale=-1.0), f"dg{t}")
            for x, dst in enumerate((DQ, DK, DV)):
                for t in range(T):
                    bk = wait_full(act, f"ct{x}{t}")
                    done(copy(dst[:, t * 512:(t + 1) * 512], bk[:, :]), f"ct{x}{t}")
            for t in range(T):
                bk = wait_full(act, f"aT0{t}")
                done(A(v3(aqkT[:, 0:1024], 4)[:, :, t * P:(t + 1) * P], v3(bk[:, :], 4), ACT.Copy, scale=qg8), f"aT0{t}")
            for h in range(AH):
                act.wait_ge(S["a_max"], h + 1)
                bk = wait_full(act, f"as{h}")
                step(A(aP[:, h, 0:P], bk[:, 0:P], ACT.Exp, bias=a_mx[:, 2 * h:2 * h + 1],
                       accum_out=a_sum[:, 2 * h:2 * h + 1]))
                step(A(aP[:, h, P:384], bk[:, P:384], ACT.Exp, bias=a_mx[:, 2 * h + 1:2 * h + 2],
                       accum_out=a_sum[:, 2 * h + 1:2 * h + 2]))
                act.sem_inc(S["a_exp"], 1)
                act.sem_inc(read[where[f"as{h}"][0]], 1)
            for h in range(0, AH, 2):
                bk = wait_full(act, f"apT{h}")
                done(copy(aPT[:, h, :], bk[:, 0:384]), f"apT{h}")
            act.wait_ge(S["dn_ss"], 1)
            inv_rms(n_rs, n_ss, 16, 1).then_inc(S["dn_rs"], 1)
            act.wait_ge(S["dec_ready"], 1)
            step(A(edec, dec[:, 0:8], ACT.Exp))
            step(A(ecd, dec[:, 16:32], ACT.Exp))
            A(etl, t1, ACT.Exp).then_inc(S["dec_exp"], 1)
            for t in range(T):
                act.wait_ge(S["et_req"], t + 1)
                A(ET[:, t * 512:(t + 1) * 512], ET[:, t * 512:(t + 1) * 512], ACT.Exp).then_inc(S["et_exp"], 1)
            for x, dst in enumerate((kT, kbT, qT, qdT)):
                for t in range(T):
                    bk = wait_full(act, f"dT{x}{t}")
                    done(copy(dst[:, t * 512:(t + 1) * 512], bk[:, :]), f"dT{x}{t}")
            for t in range(T):
                bk = wait_full(act, f"D0{t}")
                done(copy(DI[:, t * 512:(t + 1) * 512], bk[:, :]), f"D0{t}")
            for l in range(len(LEVELS)):
                for t in range(T):
                    bk = wait_full(act, f"Y{l}{t}")
                    done(copy(YY[:, t * 512:(t + 1) * 512], bk[:, :]), f"Y{l}{t}")
            for t in range(T):
                bk = wait_full(act, f"val{t}")
                done(copy(VAL[:, t * 512:(t + 1) * 512], bk[:, :]), f"val{t}")
                bk = wait_full(act, f"kc{t}")
                done(copy(KC[:, t * 512:(t + 1) * 512], bk[:, :]), f"kc{t}")
            for n in range(4):
                t, r = n // 2, C * (n % 2)
                bk = wait_full(act, f"do{n}")
                done(copy(odn[r:r + C, t * 512:(t + 1) * 512], bk[r:r + C, :]), f"do{n}")
            act.wait_ge(S["o_ss"], 1)
            step(A(lnv[:, 0:8], n_ss[:, 0:8], ACT.Ln, scale=1.0 / DD, bias=EPSC))
            step(A(n_rs[:, 0:8], lnv[:, 0:8], ACT.Exp, scale=-0.5))
            inv_rms(rstd, ss, T, 512).then_inc(S["o_rs"], 1)
            evac_T("oT")
            act.wait_ge(S["x1_new"], 4)
            norm("n2")
            evac_T("n2T")
            for c in range(16):
                bk = wait_full(act, f"z{c}")
                if c >= 2:
                    act.wait_ge(S["z_done"], c - 1)
                done(A(zr[:, (c % 2) * 512:(c % 2 + 1) * 512], bk[:, :], ACT.Relu), f"z{c}")
            act.wait_ge(S["x2_new"], 4)
            norm("n3")
            evac_T("n3T")
            def rope_evac(x):
                for t in range(T):
                    bk = wait_full(act, f"rT{x}{t}")
                    done(copy(qkT2[:, x, :, t * P:(t + 1) * P], v3(bk[:, :], 4)), f"rT{x}{t}")

            ROPE = {0: 0, 1: 1, 6: 2, 7: 3, 8: 4, 9: 5}
            pend = []
            for c in range(16):
                for t in range(T):
                    n = f"p{c}_{t}"
                    o = t * 1024 + (c % 2) * 512
                    if c in (2, 3, 10, 11):
                        bk = wait_full(act, n)
                        done(copy((RVt if c < 4 else DVt)[:, o:o + 512], bk[:, :]), n)
                    elif c in (4, 5):
                        bk = wait_full(act, n)
                        step(copy(RG[:, o:o + 512], bk[:, :]))
                        i = 2 * (c - 4) + t
                        if i >= 2:
                            act.wait_ge(S["gate2"], i - 1)
                        A(gex[:, t * 512:(t + 1) * 512], bk[:, :], ACT.Exp, scale=-1.0).then_inc(S["g_exp"], 1)
                        act.wait_ge(S["g_exp"], i + 1)
                        act.sem_inc(read[where[n][0]], 1)
                    elif c >= 12:
                        bk = wait_full(act, n)
                        done(A((GR if c < 14 else GD)[:, o:o + 512], bk[:, :], ACT.Exp, scale=-1.0), n)
                for x in pend:
                    rope_evac(x)
                pend = [ROPE[c]] if c in ROPE else []
            for hh in range(2):
                bk = wait_full(act, f"kv{hh}")
                done(copy(KV[:, hh * 512:(hh + 1) * 512], bk[:, :]), f"kv{hh}")
            for t in range(T):
                for hh in range(2):
                    bk = wait_full(act, f"ro{t}{hh}")
                    done(copy(tok[:, t * 1024 + hh * 512:t * 1024 + (hh + 1) * 512], bk[:, :]), f"ro{t}{hh}")
            act.wait_ge(S["head_ss"], 1)
            inv_rms(n_rs[:, 0:8], n_ss[:, 0:8], 8, RV).then_inc(S["head_rs"], 1)
            for x in range(8):
                act.wait_ge(S["p_max"], x + 1)
                bk = wait_full(act, f"ps{x}")
                step(A(P2[:, x, 0:P], bk[:, 0:P], ACT.Exp, scale=RK ** -0.5, bias=a_mx[:, 2 * x:2 * x + 1],
                       accum_out=a_sum[:, 2 * x:2 * x + 1]))
                step(A(P2[:, x, P:384], bk[:, P:384], ACT.Exp, scale=RK ** -0.5, bias=a_mx[:, 2 * x + 1:2 * x + 2],
                       accum_out=a_sum[:, 2 * x + 1:2 * x + 2]))
                act.sem_inc(S["p_exp"], 1)
                act.sem_inc(read[where[f"ps{x}"][0]], 1)
            evac_T("rtT")
            for h in range(0, RH, 2):
                bk = wait_full(act, f"pT{h}")
                done(copy(PT2[:, h, :], bk[:, 0:384]), f"pT{h}")
            for t in range(T):
                for hh in range(2):
                    bk = wait_full(act, f"po{t}{hh}")
                    done(copy(tok[:, t * 1024 + hh * 512:t * 1024 + (hh + 1) * 512], bk[:, :]), f"po{t}{hh}")
            act.wait_ge(S["head_ss"], 2)
            inv_rms(n_rs[:, 0:8], n_ss[:, 0:8], 8, RV).then_inc(S["head_rs"], 1)
            evac_T("dtT")
            for x in range(4):
                bk = wait_full(act, f"gr{x}")
                done(copy((grow1 if x < 2 else grow2)[:, (x % 2) * 512:(x % 2 + 1) * 512], bk[:, :]), f"gr{x}")
            evac_T("mT")
            act.wait_ge(S["x3_new"], 4)
            norm("n4")
            evac_T("n4T")
            act.wait_ge(S["router_req"], 1)
            A(rt[:, 0:8], rt[:, 0:8], ACT.Exp).then_inc(S["router_exp"], 1)
            act.wait_ge(S["router_req"], 2)
            A(rs8[:, 8:10], rs8[:, 8:10], ACT.Exp).then_inc(S["router_exp"], 1)
            with act.Fori(0, E // 2) as it:
                for u in range(2):
                    act.wait_ge(S["hid_done"], 2 * it + u + 1)
                    for hh in range(2):
                        act.wait_ge(full[hh], base[hh] + 2 * it + u + 1)
                        A(hex_[:, hh * 512:(hh + 1) * 512], banks[hh][:, :], ACT.Exp, scale=-1.0).then_inc(S["e_exp"], 1)
            act.wait_ge(S["y_done"], 1)
            norm("n5")
            act.wait_ge(S["out_done"], 1)
            for t in range(T):
                act.dma_start(out[0, t * P:(t + 1) * P, :], tok3[:, t, :]).then_inc(S["store"], 16)
            act.wait_ge(S["store"], 16 * T)

        @block.vector
        def _(dve):
            V = nc.vector
            TS, TT, STT = V.tensor_scalar, V.tensor_tensor, V.scalar_tensor_tensor

            def step(ins):
                chain(dve, ins, "dve_step")

            def tt(o, a, b, op):
                step(TT(o, a, b, op))

            def norm_tok(name):
                dve.wait_ge(S[f"{name}_rs"], 1)
                for t in range(T):
                    TS(tok3[:, t, :], X3[:, t, :], rstd[:, t:t + 1], None, ALU.mult).then_inc(S[f"{name}_tok"], 1)

            def evac_T(name):
                for j in (1, 3):
                    bk = wait_full(dve, f"{name}{j}")
                    for k in range(2):
                        sc, bi = GAIN[name](2 * j + k)
                        o = aT[:, 2 * j + k, :]
                        p = bk[:, k * 256:(k + 1) * 256]
                        if sc is None:
                            i = V.tensor_copy(o, p)
                        elif bi is None:
                            i = TS(o, p, sc, None, ALU.mult)
                        else:
                            i = TS(o, p, sc, bi, ALU.mult, ALU.add)
                    done(i, f"{name}{j}")

            V.memset(EPSC, EPS).then_inc(S["eps_set"], 1)
            dve.wait_ge(S["pos_in"], 16)
            dve.wait_ge(S["const_in"], 16)
            step(V.tensor_copy(posf, posi[:, :]))
            a4, k4 = v3(angle[:, :], 4), v3(angk[:, :], 4)
            for x in range(4):
                step(TS(a4[:, x, :], K("inv"), posf[:, x % 2:x % 2 + 1], None, ALU.mult))
            step(TS(angk[:, 0:128], angle[:, 0:128], 1 / (2 * np.pi), 0.25, ALU.mult, ALU.add))
            step(TS(angk[:, 128:256], angle[:, 128:256], 1 / (2 * np.pi), None, ALU.mult))
            step(TS(angk[:, :], angk[:, :], 12582912.0, None, ALU.add))
            step(TS(angk[:, :], angk[:, :], -12582912.0, None, ALU.add))
            for cw in (6.28125, 0.0019350051879882812, 3.0199159819e-7):
                step(STT(angle[:, :], angk[:, :], -cw, angle[:, :], ALU.mult, ALU.add))
            step(TS(angle[:, 0:128], angle[:, 0:128], float(np.pi / 2), None, ALU.add))
            TS(angle[:, :], angle[:, :], 3.1415925, -3.1415925, ALU.min, ALU.max).then_inc(S["ang_ready"], 1)
            norm_tok("n1")
            wait_read(dve, "cols")
            evac_T("n1T")
            step(TS(qg8, col("qg"), AD ** -0.5, None, ALU.mult))
            step(TS(dng, col("dnorm", 0, 2), 1.0 - LAMI, None, ALU.mult))
            l2 = colA[:, colat["lam"]:colat["lam"] + 4].rearrange("p (a b) -> p b a", b=2)
            TT(lamp, l2[:, 0, :], l2[:, 1, :], ALU.mult).then_inc(S["lam_prod"], 1)
            dve.wait_ge(S["c_exp"], 1)
            step(TS(cex, cex, 1.0, None, ALU.add))
            step(V.reciprocal(cex, cex))
            TT(cs, cex, col("c", 0, 8), ALU.mult).then_inc(S["c_silu"], 1)
            dve.wait_ge(S["cin_zero"], 1)
            for x in range(3):
                for f in range(4 * x, 4 * x + 4):
                    if f % 2 == 0:
                        wait_read(dve, f"dp{x}_{(f % 4) // 2}")
                    step(TS(cout[:, f, :], cin[:, f, 0:256], colB[:, f:f + 1], None, ALU.mult))
                    for j in range(1, 4):
                        i = STT(cout[:, f, :], cin[:, f, j:j + 256], colB[:, j * 12 + f:j * 12 + f + 1],
                                cout[:, f, :], ALU.mult, ALU.add)
                        if f % 4 < 3 or j < 3:
                            step(i)
                i.then_inc(S["conv_y"], 1)
                dve.wait_ge(S["conv_e"], x + 1)
                step(TS(cexp, cexp, 1.0, None, ALU.add))
                step(V.reciprocal(cexp, cexp))
                TT(cout[:, 4 * x:4 * x + 4, :], cout[:, 4 * x:4 * x + 4, :], v3(cexp, 4), ALU.mult)\
                    .then_inc(S["conv_done"], 1)
                dve.wait_ge(S["conv_done"], x + 1)
            bk = wait_full(dve, "dadb")
            done(V.tensor_copy(dadb, bk[:, 0:16]), "dadb")
            wait_read(dve, "dadb")
            tt(v3(t1, 2), v3(dadb, 2)[:, :, 0:4], bm(dtb, 2), ALU.add)
            STT(t2, t1, -1.0, t1, ALU.mult, ALU.max).then_inc(S["gl_req"], 1)
            dve.wait_ge(S["gl_exp"], 1)
            step(STT(gl, t1, 0.0, t3, ALU.max, ALU.add))
            tt(v3(gl, 2), v3(gl, 2), bm(ea, 2), ALU.mult)
            step(TS(beta, beta, 1.0, None, ALU.add))
            step(V.reciprocal(beta, beta))
            step(TS(gl, gl, -1.0, None, ALU.mult))
            TT(v3(ghalf, 2), bm(gl, 2), bc(K("half"), 8), ALU.mult).then_inc(S["g_ready"], 1)
            for x in range(2):
                for t in range(T):
                    wait_read(dve, f"{'ak' if x else 'aq'}{t}")
                    q = v3(qktok, 4)[:, 2 * x + t, :]
                    s = v3(asq, 4)[:, 2 * x + t, :]
                    tt(s, q, q, ALU.mult)
                    o = (2 * x + t) * AH
                    V.tensor_reduce(a_ss[:, o:o + AH], v3(s, AH), AX.X, ALU.add).then_inc(S["a_ss"], 1)
            dve.wait_ge(S["a_rs"], 1)
            for xt in range(4):
                q = v3(v3(qktok, 4)[:, xt, :], AH)
                TT(q, q, bc(a_rs[:, xt * AH:(xt + 1) * AH], AD), ALU.mult).then_inc(S["a_qn"], 1)
            for t in range(T):
                wait_read(dve, f"dg{t}")
            step(TS(gexp, gexp, 1.0, None, ALU.add))
            step(V.reciprocal(gexp, gexp))
            tt(gate, gate, gexp, ALU.mult)
            for t in range(T):
                bk = wait_full(dve, f"aT1{t}")
                done(TS(v3(aqkT[:, 1024:2048], 4)[:, :, t * P:(t + 1) * P], v3(bk[:, :], 4), col("kg"), None, ALU.mult), f"aT1{t}")
            bk = wait_full(dve, "mod")
            done(TT(modc, bk[:, 0:48], col("bada", 0, 48), ALU.add), "mod")
            wait_read(dve, "mod")
            step(STT(sc1, modc[:, 8:16], 1.0, col("nmix", 0, 8), ALU.add, ALU.mult))
            step(STT(sc2, modc[:, 32:40], 1.0, col("nffn", 0, 8), ALU.add, ALU.mult))
            for h in range(AH):
                bk = wait_full(dve, f"as{h}")
                step(V.tensor_reduce(a_mx[:, 2 * h:2 * h + 1], bk[:, 0:P], AX.X, ALU.max, negate=True))
                V.tensor_reduce(a_mx[:, 2 * h + 1:2 * h + 2], bk[:, P:384], AX.X, ALU.max, negate=True)\
                    .then_inc(S["a_max"], 1)
            dve.wait_ge(S["a_exp"], AH)
            for h in range(1, AH, 2):
                bk = wait_full(dve, f"apT{h}")
                done(V.tensor_copy(aPT[:, h, :], bk[:, 0:384]), f"apT{h}")
            step(V.reciprocal(a_rd, a_sum))
            for t in range(T):
                bk = wait_full(dve, f"ao{t}")
                done(TT(v3(oatt[:, t * 512:(t + 1) * 512], AH), v3(bk[:, :], AH),
                        bc(a_rd.rearrange("p (h t) -> p t h", t=2)[:, t, :], AD), ALU.mult), f"ao{t}")
                wait_read(dve, f"ao{t}")
            for x, src in enumerate((DQ, DK)):
                for t in range(T):
                    wait_read(dve, f"ct{x}{t}")
                tt(dsq, src, src, ALU.mult)
                i = V.tensor_reduce(n_ss[:, 8 * x:8 * x + 8], v3(dsq, 8), AX.X, ALU.add)
                if x == 0:
                    step(i)
            i.then_inc(S["dn_ss"], 1)
            TT(v3(YY, 8), bm(K("cumT"), 8), bc(gl, P), ALU.mult).then_inc(S["cumg"], 1)
            bk = wait_full(dve, "dec")
            done(V.tensor_copy(dec, bk[:, 0:32]), "dec")
            wait_read(dve, "dec")
            TT(t1, dec[:, 8:16], dec[:, 0:8], ALU.subtract).then_inc(S["dec_ready"], 1)
            for t in range(T):
                bk = wait_full(dve, f"R{t}")
                e = v3(ET[:, t * 512:(t + 1) * 512], 4)
                done(TT(e, v3(bk[:, :], 4), bc(dec[:, 4 * t:4 * t + 4], P), ALU.subtract), f"R{t}")
                wait_read(dve, f"R{t}")
                TT(e, e, bm(K("negT"), 4), ALU.add).then_inc(S["et_req"], 1)
            dve.wait_ge(S["dn_rs"], 1)
            step(TS(n_rs[:, 0:8], n_rs[:, 0:8], DD ** -0.5, None, ALU.mult))
            TT(v3(DK, 8), v3(DK, 8), bc(n_rs[:, 8:16], P), ALU.mult).then_inc(S["dscaled"], 1)
            dve.wait_ge(S["dscaled"], 1)
            TT(v3(KB, 8), v3(DK, 8), bc(beta, P), ALU.mult).then_inc(S["dscaled"], 1)
            TT(v3(DQ, 8), v3(DQ, 8), bc(n_rs[:, 0:8], P), ALU.mult).then_inc(S["dscaled"], 1)
            dve.wait_ge(S["dec_exp"], 1)
            dve.wait_ge(S["dscaled"], 3)
            TT(v3(QD, 8), v3(DQ, 8), bc(edec, P), ALU.mult).then_inc(S["dscaled"], 1)
            tt(v3(KBE, 8), v3(KB, 8), bc(edec, P), ALU.mult)
            tt(v3(KTL, 8), v3(DK, 8), bc(etl, P), ALU.mult)
            for t in range(T):
                wait_read(dve, f"ct2{t}")
            tt(v3(DV, 8), v3(DV, 8), bc(beta, P), ALU.mult)
            for x, dst in enumerate((AT, MT)):
                for t in range(T):
                    dve.wait_ge(S["et_exp"], t + 1)
                    bk = wait_full(dve, f"kk{x}{t}")
                    o = slice(t * 512, (t + 1) * 512)
                    done(TT(dst[:, o], bk[:, :], ET[:, o], ALU.mult), f"kk{x}{t}")
                    wait_read(dve, f"kk{x}{t}")
                    if x == 0:
                        tt(v3(DT[:, o], 4), v3(AT[:, o], 4), bm(K("lvl1"), 4), ALU.mult)
                        TT(v3(DT[:, o], 4), v3(DT[:, o], 4), bm(ident, 4), ALU.add).then_inc(S["d_init"], 1)
            for l, s in enumerate(LEVELS):
                for t in range(T):
                    o = slice(t * 512, (t + 1) * 512)
                    if s != LEVELS[-1]:
                        bk = wait_full(dve, f"Dn{l}{t}")
                        wait_full(dve, f"Dt{l}{t}")
                        done(TT(DI[:, o], bk[:, :], DI[:, o], ALU.add), f"Dn{l}{t}")
                        wait_read(dve, f"Dn{l}{t}")
                    bk = wait_full(dve, f"Dt{l}{t}")
                    done(TT(DT[:, o], bk[:, :], DT[:, o], ALU.add), f"Dt{l}{t}")
                    wait_read(dve, f"Dt{l}{t}")
            for x in (0, 1):
                wait_read(dve, f"val{x}")
            for n in range(4):
                t, r = n // 2, C * (n % 2)
                rows = slice(r, r + C)
                o = slice(t * 512, (t + 1) * 512)
                if n == 0:
                    V.tensor_copy(VN[rows, o], VAL[rows, o]).then_inc(S["vn_new"], 1)
                else:
                    bk = wait_full(dve, f"vp{n}")
                    TT(VN[rows, o], VAL[rows, o], bk[rows, :], ALU.subtract).then_inc(S["vn_new"], 1)
                    dve.wait_ge(S["vn_new"], n + 1)
                    dve.sem_inc(read[where[f"vp{n}"][0]], 1)
                if n < 3:
                    bk = wait_full(dve, f"sn{n}")
                    if n == 0:
                        step(V.tensor_copy(ST, bk[:, :]))
                    else:
                        wait_full(dve, f"do{n}")
                        for h in range(DH):
                            hs = slice(h * P, (h + 1) * P)
                            step(STT(ST[:, hs], ST[:, hs], ecd[:, 8 * (n % 2) + 4 * t + h:8 * (n % 2) + 4 * t + h + 1],
                                     bk[:, hs], ALU.mult, ALU.add))
                    dve.sem_inc(S["s_new"], 1)
                    dve.sem_inc(read[where[f"sn{n}"][0]], 1)
            for n in range(4):
                wait_read(dve, f"do{n}")
            tt(dsq, odn, odn, ALU.mult)
            step(V.tensor_reduce(n_ss[:, 0:8], v3(dsq, 8), AX.X, ALU.add))
            tt(dsq, oatt, oatt, ALU.mult)
            V.tensor_reduce(ss, v3(dsq, 2), AX.X, ALU.add).then_inc(S["o_ss"], 1)
            dve.wait_ge(S["o_rs"], 1)
            tt(v3(odn, 8), v3(odn, 8), bc(n_rs[:, 0:8], P), ALU.mult)
            tt(tok3[:, :, 512:1024], v3(odn, 2), v3(gate, 2), ALU.mult)
            TT(tok3[:, :, 0:512], v3(oatt, 2), bc(rstd, 512), ALU.mult).then_inc(S["o_tok"], 1)
            evac_T("oT")

            def add_x(name, c, t, sem):
                bk = wait_full(dve, name)
                xs = X3[:, t, c * 512:(c + 1) * 512]
                TT(xs, bk[:, :], xs, ALU.add).then_inc(S[sem], 1)
                return bk

            for c in range(2):
                for t in range(T):
                    add_x(f"mo{c}{t}", c, t, "x1_new")
                    dve.wait_ge(S["x1_new"], 2 * c + t + 1)
                    dve.sem_inc(read[where[f"mo{c}{t}"][0]], 1)
            norm_tok("n2")
            evac_T("n2T")
            for c in range(16):
                wait_read(dve, f"z{c}")
                z = v3(zr[:, (c % 2) * 512:(c % 2 + 1) * 512], 2)
                TT(zT[:, 2 * c:2 * c + 2, :], z, z, ALU.mult).then_inc(S["z_done"], 1)
            for j in range(4):
                add_x(f"y{j}", j % 2, j // 2, "x2_new")
                dve.wait_ge(S["x2_new"], j + 1)
                dve.sem_inc(read[where[f"y{j}"][0]], 1)
            norm_tok("n3")
            evac_T("n3T")
            ROPE = {0: 0, 1: 1, 6: 2, 7: 3, 8: 4, 9: 5}
            dve.wait_ge(S["ang_done"], 1)
            for c in range(16):
                for t in range(T):
                    n = f"p{c}_{t}"
                    o = t * 1024 + (c % 2) * 512
                    if c in ROPE:
                        x = ROPE[c]
                        bk = wait_full(dve, n)
                        cos, sin = cosin[:, t * 64:(t + 1) * 64], cosin[:, 128 + t * 64:128 + (t + 1) * 64]
                        step(TT(v3(ropeA, 8), v3(bk[:, :], 8), bm(cos, 8), ALU.mult))
                        done(TT(v3(ropeB, 8), v3(bk[:, :], 8), bm(sin, 8), ALU.mult), n)
                        wait_read(dve, n)
                        A4, B4 = (r.rearrange("p (h a n) -> p h a n", h=4, a=2) for r in (ropeA, ropeB))
                        O4 = ropeO[:, t * 512:(t + 1) * 512].rearrange("p (h a n) -> p h a n", h=4, a=2)
                        if x:
                            wait_full(dve, f"rT{x - 1}{t}")
                        if x == 2 and t == 0:
                            dve.wait_ge(S["kz_done"], 1)
                        tt(O4[:, :, 0, :], A4[:, :, 0, :], B4[:, :, 1, :], ALU.subtract)
                        TT(O4[:, :, 1, :], A4[:, :, 1, :], B4[:, :, 0, :], ALU.add).then_inc(S["rope_out"], 1)
                        dve.wait_ge(S["rope_out"], 2 * x + t + 1)
                        if x == 1 and t == 0:
                            TT(v3(KZ, 4), v3(ropeO[:, 0:512], 4), bc(K("zeta"), P), ALU.mult).then_inc(S["kz_done"], 1)
                    elif c in (4, 5):
                        i = 2 * (c - 4) + t
                        dve.wait_ge(S["g_exp"], i + 1)
                        gx = gex[:, t * 512:(t + 1) * 512]
                        step(TS(gx, gx, 1.0, None, ALU.add))
                        step(V.reciprocal(gx, gx))
                        TT(RG[:, o:o + 512], RG[:, o:o + 512], gx, ALU.mult).then_inc(S["gate2"], 1)
                        dve.wait_ge(S["gate2"], i + 1)
                    elif c >= 12:
                        wait_read(dve, n)
                        gt = (GR if c < 14 else GD)[:, o:o + 512]
                        step(TS(gt, gt, 1.0, None, ALU.add))
                        step(V.reciprocal(gt, gt))

            for t in range(T):
                bk = wait_full(dve, f"rs{t}")
                TT(sT[:, t * 512:(t + 1) * 512], bk[:, :], K("dmaskT"), ALU.mult).then_inc(S["st_done"], 1)
                dve.wait_ge(S["st_done"], t + 1)
                dve.sem_inc(read[where[f"rs{t}"][0]], 1)
            for hh in range(2):
                wait_read(dve, f"ro1{hh}")
                bk = wait_full(dve, f"rx{hh}")
                for h in range(2):
                    hd = 2 * hh + h
                    o = tok[:, 1024 + hd * 256:1024 + (hd + 1) * 256]
                    i = STT(o, bk[:, h * 256:(h + 1) * 256], K("xi")[:, hd:hd + 1], o, ALU.mult, ALU.add)
                done(i, f"rx{hh}")
                wait_read(dve, f"rx{hh}")

            def head_norm(i):
                tt(sq2, tok[:, :], tok[:, :], ALU.mult)
                V.tensor_reduce(n_ss[:, 0:8], v3(sq2, 8), AX.X, ALU.add).then_inc(S["head_ss"], 1)
                dve.wait_ge(S["head_rs"], i + 1)

            for hh in range(2):
                wait_read(dve, f"ro0{hh}")
            head_norm(0)
            tt(v3(tok[:, :], 8), v3(tok[:, :], 8), bc(n_rs[:, 0:8], RV), ALU.mult)
            for t in range(T):
                TT(tok3[:, t, :], tok3[:, t, :], RG[:, t * 1024:(t + 1) * 1024], ALU.mult).then_inc(S["r_tok"], 1)
            for x in range(8):
                bk = wait_full(dve, f"ps{x}")
                step(V.tensor_reduce(a_mx[:, 2 * x:2 * x + 1], bk[:, 0:P], AX.X, ALU.max, negate=True))
                step(V.tensor_reduce(a_mx[:, 2 * x + 1:2 * x + 2], bk[:, P:384], AX.X, ALU.max, negate=True))
                TS(a_mx[:, 2 * x:2 * x + 2], a_mx[:, 2 * x:2 * x + 2], RK ** -0.5, None, ALU.mult)\
                    .then_inc(S["p_max"], 1)
            dve.wait_ge(S["p_exp"], 8)
            evac_T("rtT")
            wait_read(dve, "lam")
            step(STT(lam, lame[:, 0:1], LAMI, lame[:, 1:2], ALU.add, ALU.subtract))
            step(V.reciprocal(a_rd, a_sum))
            a4v = a_rd.rearrange("p (h c t) -> p h c t", h=4, c=2)
            step(TS(a4v[:, :, 1, :], a4v[:, :, 1, :], lam, None, ALU.mult))
            for h in range(RH):
                for r in range(2):
                    w = slice(0, P) if r == 0 else slice(P, 384)
                    j = 4 * h + r
                    step(TS(P2[:, 2 * h + 1, w], P2[:, 2 * h + 1, w], a_rd[:, j + 2:j + 3], None, ALU.mult))
                    i = STT(P2[:, 2 * h, w], P2[:, 2 * h, w], a_rd[:, j:j + 1], P2[:, 2 * h + 1, w], ALU.mult, ALU.subtract)
                    if r == 0:
                        step(i)
                i.then_inc(S["a_done"], 1)
            for c in range(2):
                for t in range(T):
                    n = f"rp{c}{t}"
                    bk = wait_full(dve, n)
                    o = slice(t * 1024 + c * 512, t * 1024 + (c + 1) * 512)
                    done(TT(GR[:, o], bk[:, :], GR[:, o], ALU.mult), n)
            for h in range(1, RH, 2):
                bk = wait_full(dve, f"pT{h}")
                done(V.tensor_copy(PT2[:, h, :], bk[:, 0:384]), f"pT{h}")
            for t in range(T):
                for hh in range(2):
                    wait_read(dve, f"po{t}{hh}")
            head_norm(1)
            for t in range(T):
                TT(v3(tok3[:, t, :], 4), v3(tok3[:, t, :], 4), bc(n_rs[:, 4 * t:4 * t + 4], RV), ALU.mult)\
                    .then_inc(S["r_tok"], 1)
            evac_T("dtT")
            step(TT(v3(gdiag[:, 0:1024], 8), bm(ident, 8), bc(modc[:, 16:24], P), ALU.mult))
            TT(v3(gdiag[:, 1024:2048], 8), bm(ident, 8), bc(modc[:, 40:48], P), ALU.mult).then_inc(S["diag"], 1)
            for c in range(2):
                for t in range(T):
                    n = f"wd{c}{t}"
                    bk = wait_full(dve, n)
                    o = slice(t * 1024 + c * 512, t * 1024 + (c + 1) * 512)
                    done(TT(GD[:, o], bk[:, :], GD[:, o], ALU.mult), n)
                    wait_read(dve, n)
                    i = TT(GR[:, o], GR[:, o], GD[:, o], ALU.add)
            i.then_inc(S["m_done"], 1)
            evac_T("mT")
            for x in range(4):
                wait_read(dve, f"gr{x}")
            for c in range(2):
                for t in range(T):
                    n = f"xo{c}{t}"
                    bk = wait_full(dve, n)
                    o = tok3[:, t, c * 512:(c + 1) * 512]
                    xs = X3[:, t, c * 512:(c + 1) * 512]
                    done(TT(o, bk[:, :], grow1[:, c * 512:(c + 1) * 512], ALU.mult), n)
                    wait_read(dve, n)
                    TT(xs, xs, o, ALU.add).then_inc(S["x3_new"], 1)
            norm_tok("n4")
            evac_T("n4T")
            bk = wait_full(dve, "rout")
            done(TT(v3(lg[:, :], 2), v3(bk[:, 0:72], 2), bm(rbias, 2), ALU.add), "rout")
            wait_read(dve, "rout")
            l2 = v3(lg[:, :], 2)
            G, EL = l2[:, :, 0:4], l2[:, :, 4:36]
            gm, gs, gtop, m1, m2, w1, w2 = (rs8[:, 2 * i:2 * i + 2] for i in (0, 1, 2, 3, 5, 6, 7))
            e2 = rs8[:, 8:10]
            r4, hot4 = v3(rt[:, 0:8], 2), v3(rt[:, 8:16], 2)
            pr4 = K("prio")[:, 28:32]
            step(V.tensor_reduce(gm, G, AX.X, ALU.max))
            TT(r4, G, bc(gm, 4), ALU.subtract).then_inc(S["router_req"], 1)
            tt(hot4, G, bc(gm, 4), ALU.is_equal)
            tt(hot4, hot4, bm(pr4, 2), ALU.mult)
            step(V.tensor_reduce(m1, hot4, AX.X, ALU.max))
            tt(hot4, hot4, bc(m1, 4), ALU.is_equal)
            step(TS(hot4, hot4, -1.0, -NEG, ALU.add, ALU.mult))
            mel = rt2[:, 0:64]
            step(V.tensor_copy(v3(mel, 2), EL))
            tt(v3(mel, 8), v3(mel, 8), bc(rt[:, 8:16], EG), ALU.add)
            h1, h2 = v3(rt3[:, 0:64], 2), v3(Wt[:, :], 2)

            def first_best(h, m):
                step(V.tensor_reduce(m, v3(mel, 2), AX.X, ALU.max))
                tt(h, v3(mel, 2), bc(m, E), ALU.is_equal)
                tt(h, h, bm(K("prio"), 2), ALU.mult)
                step(V.tensor_reduce(gm, h, AX.X, ALU.max))
                tt(h, h, bc(gm, E), ALU.is_equal)

            first_best(h1, m1)
            step(STT(mel, rt3[:, 0:64], 3 * NEG, mel, ALU.mult, ALU.add))
            first_best(h2, m2)
            TT(e2, m2, m1, ALU.subtract).then_inc(S["router_req"], 1)
            dve.wait_ge(S["router_exp"], 2)
            step(V.tensor_reduce(gs, r4, AX.X, ALU.add))
            step(V.reciprocal(gtop, gs))
            step(TS(w1, e2, 1.0, None, ALU.add))
            step(V.reciprocal(w1, w1))
            tt(w1, w1, gtop, ALU.mult)
            tt(w2, w1, e2, ALU.mult)
            tt(h1, h1, bc(w1, E), ALU.mult)
            tt(h2, h2, bc(w2, E), ALU.mult)
            tt(h2, h2, h1, ALU.add)
            step(V.memset(arena[:, 0:2048], 0.0))
            dve.sem_inc(S["hid_done"], 1)
            with dve.Fori(0, E // 2) as it:
                for u in range(2):
                    def mstep(ins, i):
                        ins.then_inc(S["mo_step"], 1)
                        dve.wait_ge(S["mo_step"], 8 * it + 4 * u + i)
                    dve.wait_ge(S["e_exp"], 4 * it + 2 * u + 2)
                    mstep(TS(hex_, hex_, 1.0, None, ALU.add), 1)
                    mstep(V.reciprocal(hex_, hex_), 2)
                    for hh in range(2):
                        s = slice(hh * 512, (hh + 1) * 512)
                        dve.wait_ge(full[hh], base[hh] + 2 * it + u + 1)
                        TT(hex_[:, s], banks[hh][:, :], hex_[:, s], ALU.mult).then_inc(read[hh], 1)
                        dve.wait_ge(read[hh], base[hh] + 2 * it + u + 1)
                    dve.wait_ge(full[7], base[7] + 2 * it + u)
                    for hh in range(2):
                        s = slice(hh * 512, (hh + 1) * 512)
                        dve.wait_ge(full[2 + hh], base[2 + hh] + 2 * it + u + 1)
                        i = TT(hid[:, s], banks[2 + hh][:, :], hex_[:, s], ALU.mult)
                        i.then_inc(read[2 + hh], 1)
                        dve.wait_ge(read[2 + hh], base[2 + hh] + 2 * it + u + 1)
                    dve.sem_inc(S["hid_done"], 1)
                    mstep(TS(rs8[:, 20:21], Wt[:, bass.ds(2 * it + u, 1)], 1.0, None, ALU.mult), 3)
                    mstep(TS(rs8[:, 21:22], Wt[:, bass.ds(2 * it + (u + E), 1)], 1.0, None, ALU.mult), 4)
                    for j in range(4):
                        t, hh = j // 2, j % 2
                        ys = Y[:, t, hh * 512:(hh + 1) * 512]
                        dve.wait_ge(full[4 + j], base[4 + j] + 2 * it + u + 1)
                        STT(ys, banks[4 + j][:, :], rs8[:, 20 + t:21 + t], ys, ALU.mult, ALU.add).then_inc(read[4 + j], 1)
                        dve.wait_ge(read[4 + j], base[4 + j] + 2 * it + u + 1)
            for t in range(T):
                tt(Y[:, t, :], Y[:, t, :], G2, ALU.mult)
                i = TT(X3[:, t, :], X3[:, t, :], Y[:, t, :], ALU.add)
            i.then_inc(S["y_done"], 1)
            dve.wait_ge(S["n5_rs"], 1)
            dve.wait_ge(S["fin_in"], 16)
            for t in range(T):
                step(TS(tok3[:, t, :], X3[:, t, :], rstd[:, t:t + 1], None, ALU.mult))
                i = TT(tok3[:, t, :], tok3[:, t, :], fing, ALU.mult)
                if t == 0:
                    step(i)
            i.then_inc(S["out_done"], 1)

        @block.gpsimd
        def _(pool):
            def row_in(dst, src, sem):
                pool.dma_start(dst, src.to_broadcast([P, src.shape[1]])).then_inc(S[sem], 16)

            pool.dma_start(posi[:, :], g["positions_2"].rearrange("o (t p) -> p (o t)", p=P),
                           allow_slow_non_contiguous=True).then_inc(S["pos_in"], 16)
            row_in(dtb, g["dn_dt_bias"], "vec_in")
            row_in(alog, g["dn_a_log"], "vec_in")
            row_in(rbias[:, 0:4], g["b_router_group_2"], "vec_in")
            row_in(rbias[:, 4:36], g["b_router_expert_2"], "vec_in")
            nc.gpsimd.memset(cin[:, :, 0:3], 0.0).then_inc(S["cin_zero"], 1)
            rb = g["rel_bias"]
            for h in range(AH):
                for kt in range(2):
                    n = 256 if kt == 0 else P
                    src = bass.AP(rb.tensor, h * NREL + MAXREL - P + 1, [[1, P], [1, n]])
                    pool.dma_start(bias[:, h, kt * 256:kt * 256 + n], src).then_inc(S["bias_in"], 16)
            pool.wait_ge(S["bias_in"], 16 * 2 * AH)
            nc.gpsimd.memset(bias[0:C, :, 0:C], NEG).then_inc(S["pool_step"], 1)
            pool.wait_ge(S["pool_step"], 1)
            nc.gpsimd.memset(bias[0:C, :, 256:256 + C], NEG).then_inc(S["bias_masked"], 1)
            for l, s in enumerate(LEVELS):
                for t in range(T):
                    o = slice(t * 512, (t + 1) * 512)
                    if l == 0:
                        wait_read(pool, f"kk0{t}")
                    else:
                        wait_full(pool, f"Y{l - 1}{t}")
                    nc.gpsimd.tensor_tensor(v3(AM[:, o], 4), v3(AT[:, o], 4), bm(K(f"lvl{s}"), 4), ALU.mult)\
                        .then_inc(S["am_ready"], 1)
            pool.wait_ge(S["diag"], 1)
            pool.dma_start(wr[:, :, 0:4], g["w_router_group_2"][0].rearrange("(k p) n -> p k n", p=P)).then_inc(S["wr_in"], 16)
            pool.dma_start(wr[:, :, 4:36], g["w_router_expert_2"][0].rearrange("(k p) n -> p k n", p=P)).then_inc(S["wr_in"], 16)
            row_in(fing, g["norm_final_2"].rearrange("(o n) -> o n", o=1), "fin_in")
            pool.wait_ge(S["fin_in"], 16)
            pool.wait_ge(S["wr_in"], 32)

        @block.sync
        def _(sp):
            def src_of(kind, c):
                w = wsrc[kind][0]
                if kind == "ff2":
                    return w[c * 512:(c + 1) * 512, :].rearrange("(k p) n -> p k n", p=P)
                cols = min(WC, w.shape[1] - c * WC)
                return w[:, c * WC:c * WC + cols].rearrange("(k p) n -> p k n", p=P)

            for n, (kind, c) in enumerate(order):
                if n >= NR:
                    k0, c0 = order[n - NR]
                    if k0 == "ada" and c0 < 11:
                        sp.wait_ge(S["ada_used"], c0 + 1)
                    elif k0 == "ff2" and c0 < 7:
                        sp.wait_ge(S["ff2_used"], c0 + 1)
                    else:
                        wait_full(sp, last_job[n - NR])
                src = src_of(kind, c)
                sp.dma_start(weights(kind, c)[:, :, 0:src.shape[2]], src).then_inc(w_in[n % NR], 16)

            exps = (g["w_exp_gate_2"][0], g["w_exp_up_2"][0], g["w_exp_down_2"][0])

            def expert_load(s, e):
                m = s % 3
                w = exps[m]
                src = w[bass.ds(e, 1), :, :].rearrange("o (k p) n -> p (o k) n", p=P)
                ins = sp.dma_start(v3(mslot(s), 4 if m == 2 else KT), src)
                ins.then_inc(w_in[s] if s < NR else wx_in[s - NR], 16)

            for s in range(6):
                if s < NR:
                    wait_full(sp, last_job[NW - NR + s])
                else:
                    sp.wait_ge(S["n4_tok"], 2)
                expert_load(s, s // 3)
            with sp.Fori(0, E // 2 - 1) as it:
                for s in range(6):
                    u, m = s // 3, s % 3
                    b = (1, 3, 7)[m]
                    sp.wait_ge(full[b], base[b] + 2 * it + u + 1)
                    expert_load(s, 2 * it + (u + 2))


_INS = ("x mix_norm_gain w_in att_q_gain att_k_gain rel_bias att_out_gain dn_conv_w dn_a_log dn_dt_bias dn_out_gain "
        "w_out ffn_norm_gain w_ff1 w_ff2 c_2 positions_2 w_ada_2 b_ada_2 norm_mix_2 w_in_2 w_ret_o_2 w_diff_o_2 "
        "lam_q1_2 lam_k1_2 lam_q2_2 lam_k2_2 diff_norm_2 w_out_2 norm_ffn_2 w_router_group_2 b_router_group_2 "
        "w_router_expert_2 b_router_expert_2 w_exp_gate_2 w_exp_up_2 w_exp_down_2 norm_final_2").split()


def kernel(**inputs):
    import numpy as _np
    import concourse.bacc as _bacc
    from concourse import mybir as _mybir
    from concourse.bass_utils import run_bass_kernel_spmd as _run

    nc = _bacc.Bacc("TRN2", target_bir_lowering=False, num_devices=1)
    arrays, g = {}, {}
    for name in _INS:
        a = _np.ascontiguousarray(inputs[name])
        arrays[f"in_{name}"] = a
        g[name] = nc.dram_tensor(f"in_{name}", a.shape, _mybir.dt.from_np(a.dtype), kind="ExternalInput").ap()
    a = constants()
    arrays["in_const"] = a
    g["const"] = nc.dram_tensor("in_const", a.shape, _mybir.dt.from_np(a.dtype), kind="ExternalInput").ap()
    out = nc.dram_tensor("out_0", (1, T * P, D), _mybir.dt.float32, kind="ExternalOutput").ap()
    program(nc, g, out)
    r = _run(nc, [arrays], core_ids=[0])
    return r.results[0]["out_0"]
```

```python
import numpy as np
import concourse.bass as bass
from concourse import mybir
from contextlib import ExitStack

P = 128
T = 2
D = 1024
KT = D // P
WC = 512
SLOT = KT * WC
EPS = 1e-6
NEG = -1e30
AH, AD = 8, 64
NREL = 513
MAXREL = 256
DH, DD = 4, 128
C = 64
FF = 4096
RH, RK, RV = 4, 128, 256
E, EG, NG, DE = 32, 8, 4, 512
SL = 64
CAP = 64
NOVER = -(-(T * P - CAP) // SL)
LEVELS = [2, 4, 8, 16, 32]
THETA = 10000.0
NROWS = 18
LAMI = 0.8 - 0.6


CONST = {}


def constants():
    i = np.arange(P)
    row, col = i[:, None], i[None, :]
    same = (row // C) == (col // C)
    parts = []

    def put(name, a):
        a = np.asarray(a, np.float32).reshape(P, -1)
        CONST[name] = (sum(x.shape[1] for x in parts), a.shape[1])
        parts.append(a)

    put("ident", np.eye(P))
    put("flip", np.eye(P)[::-1])
    put("ones", np.ones((P, P)))
    put("cumT", same & (row <= col))
    put("blk", same)
    put("negT", np.where(same & (row <= col), 0.0, NEG))
    for s in [1] + LEVELS:
        m = (col // (2 * s) == row // (2 * s)) & ((col // s) % 2 == 1) & ((row // s) % 2 == 0)
        put(f"lvl{s}", -1.0 * m)
    put("causT", np.where(row <= col, 0.0, NEG))
    gamma = 1.0 - np.exp2(-5.0 - np.arange(RH, dtype=np.float32))
    logg = np.log(gamma.astype(np.float32)).astype(np.float32)
    rel = (col - row).astype(np.float32)
    dm = np.stack([np.where(rel >= 0, np.exp(logg[h] * np.maximum(rel, 0)), 0.0) for h in range(RH)], 1)
    put("dmaskT", dm * RK ** -0.5)
    put("zeta", np.exp(logg[None, :] * (P - 1 - i[:, None])) * RK ** -0.5)
    put("xi", np.exp(logg[None, :] * (i[:, None] + 1)))
    inv = (np.float32(THETA) ** (-np.arange(0, RK, 2, dtype=np.float32) / RK)).astype(np.float32)
    put("before", row < col)
    put("iota", np.broadcast_to(np.arange(SL), (P, SL)))
    put("half", np.stack([i < C, i >= C], 1))
    put("prio", np.broadcast_to(np.arange(E, 0, -1), (P, E)))
    put("inv", np.broadcast_to(inv, (P, RK // 2)))
    return np.ascontiguousarray(np.concatenate(parts, 1))


COLS = [("c", 8), ("mix", 8), ("attout", 4), ("dnout", 1), ("ffn", 8), ("nmix", 8), ("nffn", 8),
        ("dnorm", 2), ("bada", 48), ("qg", 1), ("kg", 1), ("lam", 4)]


def program(nc, g, out):
    fp32, fp32r, i32 = mybir.dt.float32, mybir.dt.float32r, mybir.dt.int32
    ALU, ACT, AX = mybir.AluOpType, mybir.ActivationFunctionType, mybir.AxisListType
    ctx = ExitStack()
    with ctx:
        base_of = {}

        def sb(name, n, dt=fp32):
            base_of[name] = -(-nc.sbuf_base // 32) * 32
            return ctx.enter_context(nc.sbuf_tensor(name, [P, n], dt))

        ncon = g["const"].shape[1]
        NR = 4
        ring = sb("ring", NR * SLOT)
        con = sb("con", ncon)
        X = sb("X", T * D)
        actT = sb("actT", KT * T * P)
        tok = sb("tok", T * D)
        rowsA = sb("rowsA", P)
        rowsB = sb("rowsB", P)
        colA = sb("colA", 104)
        colB = sb("colB", 48)
        small = sb("small", 464)
        posi = sb("posi", 2, i32)
        flagi = sb("flagi", 2, i32)
        NA = 26780
        arena = sb("arena", NA)

        def rounded(name, n, at=0):
            return nc.alloc_sbuf_tensor_at(f"{name}_r{at}", [P, n], fp32r, offset=base_of[name] + 4 * at)

        ringR, actR, tokR = rounded("ring", NR * SLOT), rounded("actT", KT * T * P), rounded("tok", T * D)
        banks = [ctx.enter_context(nc.psum_tensor(f"bank{i}", [P, 512], fp32)) for i in range(8)]

        def K(name):
            o, n = CONST[name]
            return con[:, o:o + n]

        ident, ones, flip = K("ident"), K("ones"), K("flip")
        colat, o = {}, 0
        for name, n in COLS:
            colat[name] = o
            o += n
        NCOL = o

        def col(name, i=0, n=1):
            return colA[:, colat[name] + i:colat[name] + i + n]

        at = {"n": 0}

        def sm(n):
            at["n"] += n
            assert at["n"] <= 464
            return small[:, at["n"] - n:at["n"]]

        def ar(o, n):
            assert o + n <= NA, (o, n)
            return arena[:, o:o + n]

        X3 = X[:, :].rearrange("p (t d) -> p t d", t=T)
        tok3 = tok[:, :].rearrange("p (t d) -> p t d", t=T)
        aT = actT[:, :].rearrange("p (k n) -> p k n", k=KT)

        def slot(i):
            return ring[:, (i % NR) * SLOT:(i % NR + 1) * SLOT]

        av = ar(0, 1024)
        gate = ar(1024, 1024)
        oatt = ar(2048, 1024)
        odn = ar(3072, 1024)
        DQ, DK, DV = ar(4096, 1024), ar(5120, 1024), ar(6144, 1024)
        R0 = 7168
        CW = T * P + 3
        cin = ar(R0, 12 * CW).rearrange("p (f n) -> p f n", f=12)
        cout = ar(R0 + 3200, 3072).rearrange("p (f n) -> p f n", f=12)
        cexp = ar(R0 + 6400, 1024)
        qktok = ar(R0 + 7424, 2048)
        asq = ar(R0 + 9472, 2048)
        aqkT = ar(R0 + 11520, 2048)
        bias = ar(R0 + 13568, 3072).rearrange("p (h n) -> p h n", h=AH)
        aP = ar(R0, 3072).rearrange("p (h n) -> p h n", h=AH)
        aPT = ar(R0 + 3200, 3072).rearrange("p (h n) -> p h n", h=AH)
        gexp = ar(R0 + 6400, 1024)
        KB, KBE, KTL, QD = [ar(R0 + 1024 * i, 1024) for i in range(4)]
        kT, kbT, qT, qdT = [ar(R0 + 4096 + 1024 * i, 1024) for i in range(4)]
        ET, AT, MT, DI, DT, YY, AM, VAL, KC, VN = [ar(R0 + 8192 + 1024 * i, 1024) for i in range(10)]
        ST = ar(R0 + 18432, 512)
        dsq = AM
        mrow = tok[:, 0:1536]
        csb = tok[:, 1536:1536 + KT * 32]
        zT = ar(0, 8192).rearrange("p (f n) -> p f n", f=32)
        zr = ar(8192, 1024)
        zf = ar(17408, 512)
        zTR, zTLR = (rounded("arena", 8192, o)[:, :].rearrange("p (f n) -> p f n", f=32) for o in (0, 9216))
        NH = 3
        high1 = [rounded("arena", 2048, o)[:, :] for o in (23808, 4096, 2048)]
        high = [rounded("arena", 2048, 18944 + 2048 * i)[:, :] for i in range(NH)]
        aH, aL = (x[:, :].rearrange("p (k n) -> p k n", k=KT) for x in (tokR, actR))
        qkT2 = ar(0, 6144).rearrange("p (c h n) -> p c h n", c=6, h=RH)
        RVt, DVt, RG, GR, GD = [ar(6144 + 2048 * i, 2048) for i in range(5)]
        ropeA, ropeB = ar(16384, 512), ar(16896, 512)
        ropeO = ar(17408, 1024)
        KZ = ar(18432, 512)
        sT = ar(18944, 1024)
        KV = ar(19968, 1024)
        P2 = ar(20992, 3072).rearrange("p (h n) -> p h n", h=8)
        PT2 = ar(24064, 1536).rearrange("p (h n) -> p h n", h=4)
        gex = ar(25600, 1024)
        grow1, grow2 = ar(6144, 1024), ar(7168, 1024)
        gdiag = ar(0, 2048)
        sq2 = ar(16384, 2048)
        wr = ar(4096, 8 * 36).rearrange("p (k n) -> p k n", k=KT)
        lg, rt, rt2, rt3, rs8, Wt = [ar(4400 + 72 * i, 72) for i in range(6)]
        Wt = Wt[:, 0:64]
        xg = ar(2048, 512)
        gex2, hid = ar(2560, 256), ar(2816, 256)
        hidT = ar(3072, 256)
        Pm = ar(3328, T * SL)
        PwD = [ar(3456 + 256 * i, 256) for i in range(2)]
        RW = ar(4832, 4 * (E + 1))
        cur = ar(4968, 4)
        sel = ar(4976, 64)
        flagf = ar(5040, 2)
        PT = [[ar(5100 + 256 * (2 * i + j), 256) for j in range(2)] for i in range(2)]
        ysb = ar(6124, 512)
        cnt = ar(6640, 32)
        ZT = [ar(6680, 256)] * 2
        G2 = ar(7168, 1024)
        fing = ar(8192, 1024)
        scaled = ar(0, 2048)
        XS = 9216
        xslots = [ar(XS, SLOT), ar(XS + SLOT, SLOT)]

        ss = sm(2); lnv = sm(16); rstd = sm(2)
        a_ss = sm(32); a_rs = sm(32); a_mx = sm(16); a_sum = sm(16); a_rd = sm(16)
        n_ss = sm(16); n_rs = sm(16)
        dtb = sm(4); alog = sm(4); ea = sm(4)
        dadb = sm(16); t1 = sm(8); t2 = sm(8); t3 = sm(8); gl = sm(8); beta = sm(8); dnt = sm(8)
        dec = sm(32); ghalf = sm(16); edec = sm(8); etl = sm(8); ecd = sm(16)
        cs = sm(8); cex = sm(8)
        modc = sm(48); sc1 = sm(8); sc2 = sm(8)
        EPSC = sm(1)
        posf = sm(2); dng = sm(2); qg8 = sm(1)
        lamp = sm(2); lame = sm(2); lam = sm(1)
        rbias = sm(36)
        angle, angk = ar(3072, 256), ar(3328, 256)
        cosin = sb("cosin", 4 * 64)

        names = """x_in rows_in const_in vec_in bias_in pos_in wr_in fin_in ff2_used
                 dve_step act_step pool_step n1_rs n1_tok n2_rs n2_tok n3_rs n3_tok n4_rs n4_tok n5_rs
                 cin_zero eps_set gate2 y_done conv_y conv_e conv_done dn_ss dn_rs a_ss a_rs a_qn a_max a_exp bias_masked gexp_done
                 c_exp c_silu ang_ready ang_done gl_req gl_exp g_ready cumg dec_ready dec_exp et_req et_exp
                 dscaled at_ready d_init am_ready vn_new s_new odn_ready gate_done o_ss o_rs o_tok x1_new
                 z_relu z_done x2_new rope_out kz_done st_done g_exp head_ss head_rs r_tok p_max p_exp a_done
                 lam_prod lam_exp m_done diag x3_new router_req router_exp w_moe y_zero
                 wr_free fin_free out_done store hid_step over_step
                 rank_req sel_ready rw_ready w_high w_rest half_used t_high t_rest p_ready moe_exp moe_hid moe_zero y_sum flag_ready
                 over_go over_w over_p over_x over_xg over_g over_e over_a over_t over_te over_d over_y over_sc""".split()
        S = {n: ctx.enter_context(nc.semaphore(n)) for n in names}
        w_in = [ctx.enter_context(nc.semaphore(f"w_in{i}")) for i in range(NR)]
        wx_in = [ctx.enter_context(nc.semaphore(f"wx_in{i}")) for i in range(2)]
        full = [ctx.enter_context(nc.semaphore(f"bank_full{i}")) for i in range(8)]
        read = [ctx.enter_context(nc.semaphore(f"bank_read{i}")) for i in range(8)]

        order = ([("win", c) for c in (3, 4, 5, 7, 0, 1, 2, 6)] + [("ada", c) for c in range(12)]
                 + [("wout", c) for c in range(2)]
                 + [("ff1", c) for c in range(8)] + [("ff2", c) for c in range(8)]
                 + [("win2", c) for c in range(16)]
                 + [("wret", c) for c in range(2)] + [("wdiff", c) for c in range(2)]
                 + [("wout2", c) for c in range(2)])
        NW = len(order)
        place = {k: n for n, k in enumerate(order)}
        assert NW % NR == 0
        wsrc = {"win": g["w_in"], "ada": g["w_ada_2"], "wout": g["w_out"], "ff1": g["w_ff1"], "ff2": g["w_ff2"],
                "win2": g["w_in_2"], "wret": g["w_ret_o_2"], "wdiff": g["w_diff_o_2"], "wout2": g["w_out_2"]}

        def weights(kind, c):
            s = slot(place[(kind, c)])
            return s.rearrange("p (k n) -> p k n", k=4 if kind == "ff2" else KT)

        halves = [(k, c, h) for k, n in (("win", (3, 4, 5, 0, 1, 2, 6)), ("ff1", range(8)), ("ff2", range(8)),
                                         ("win2", range(16))) for c in n for h in range(2)]
        hat = {x: i for i, x in enumerate(halves)}
        F1, W2 = hat[("ff1", 0, 0)], hat[("win2", 0, 0)]

        def by_columns(kind, c):
            return kind == "ff1" or (kind == "win" and c in (3, 4, 5))

        by_rows = [x for x in halves if not by_columns(*x[:2]) and x[2] == 0]

        def half(i, src=ring):
            kind, c, h = halves[i]
            o = place[(kind, c)] % NR * SLOT
            s = src[:, o:o + SLOT]
            hi = (high1 if i < F1 else high)[i % NH]
            if by_columns(kind, c):
                return v3(s, KT)[:, :, h * 256:(h + 1) * 256], v3(hi, KT)
            return v3(s[:, h * 2048:(h + 1) * 2048], 2), v3(hi, 2)

        def wait_used(eng, i):
            kind, c, h = halves[i]
            if by_columns(kind, c):
                wait_full(eng, f"z{2 * c + h}" if kind == "ff1" else f"dp{c - 3}_{h}")
            elif h == 0:
                eng.wait_ge(S["half_used"], by_rows.index((kind, c, h)) + 1)
            elif kind == "ff2" and c < 7:
                eng.wait_ge(S["ff2_used"], c + 1)
            else:
                wait_full(eng, last_job[place[(kind, c)]])

        SPLIT_T = {"n1T": 0, "n2T": 1, "n3T": 2}

        def mslot(s):
            return slot(s) if s < NR else xslots[s - NR]

        def moe_in(s, it):
            return (w_in[s], 16 * (NW // NR + 1) + 16 * it) if s < NR else (wx_in[s - NR], 16 + 16 * it)

        BX, BG, BH, BO = range(4)
        last_job = {}

        uses, where, base = [0] * 8, {}, [0] * 8

        def job(name):
            b = sum(uses) % 8
            uses[b] += 1
            where[name] = (b, uses[b])
            return where[name]

        def wait_full(eng, name):
            b, u = where[name]
            eng.wait_ge(full[b], u)
            return banks[b]

        def wait_read(eng, name):
            b, u = where[name]
            eng.wait_ge(read[b], u)

        def done(ins, name):
            ins.then_inc(read[where[name][0]], 1)

        def bc(ap, n):
            return ap.unsqueeze(2).to_broadcast([P, ap.shape[1], n])

        def bm(ap, k):
            return ap.unsqueeze(1).to_broadcast([P, k, ap.shape[1]])

        def v3(ap, k):
            return ap.rearrange("p (k n) -> p k n", k=k)

        block = ctx.enter_context(nc.Block())

        @block.tensor
        def _(pe):
            mm = nc.tensor.matmul

            def begin(name):
                b, u = job(name)
                if u > 1:
                    pe.wait_ge(read[b], u - 1)
                return banks[b]

            def end(ins, name):
                ins.then_inc(full[where[name][0]], 1)

            def need(kind, c):
                n = place[(kind, c)]
                pe.wait_ge(w_in[n % NR], 16 * (n // NR + 1))
                return weights(kind, c)

            def transposes(name, src):
                for j in range(4):
                    bk = begin(f"{name}{j}")
                    for k in range(2):
                        for t in range(T):
                            i = nc.tensor.transpose(bk[:, (2 * k + t) * P:(2 * k + t + 1) * P],
                                                    src[:, t, (2 * j + k) * P:(2 * j + k + 1) * P], ident)
                    end(i, f"{name}{j}")

            def wait_actT(name):
                for j in range(4):
                    wait_read(pe, f"{name}{j}")

            def tok_product(kind, c, name, cols=WC):
                w = need(kind, c)
                for t in range(T):
                    bk = begin(f"{name}{t}")
                    for k in range(KT):
                        i = mm(bk[:, 0:cols], aT[:, k, t * P:(t + 1) * P], w[:, k, 0:cols], start=(k == 0), stop=(k == KT - 1))
                    end(i, f"{name}{t}")
                last_job[place[(kind, c)]] = f"{name}1"

            def ada(n):
                for _ in range(n):
                    c = adas[0]
                    adas[0] += 1
                    if c == 0:
                        pe.wait_ge(S["c_silu"], 1)
                    w = need("ada", c)
                    bk = begin(f"mod{c}")
                    for k in range(KT):
                        for j in range(4):
                            i = mm(bk[32 * j:32 * j + 32, 0:P], csb[:, 32 * k:32 * k + 32],
                                   w[:, k, j * P:(j + 1) * P], start=(k == 0), stop=(k == KT - 1))
                    end(i, f"mod{c}")
                    last_job[place[("ada", c)]] = f"mod{c}"

            adas = [0]
            def mm3(o, l, r, start, stop):
                mm(o, l[0], r[0], start=start, stop=False)
                mm(o, l[0], r[1], start=False, stop=False)
                return mm(o, l[1], r[0], start=False, stop=stop)

            def wait_split(kind, c, h):
                pe.wait_ge(S["w_rest"], hat[(kind, c, h)] + 1)
                rest, hi = half(hat[(kind, c, h)], ringR)
                return hi, rest

            def split_product(kind, c, name):
                bks = [begin(f"{name}{t}") for t in range(T)]
                for h in range(2):
                    hi, rest = (v3(x.rearrange("p a n -> p (a n)"), 4) for x in wait_split(kind, c, h))
                    for t in range(T):
                        for k in range(4):
                            a = 4 * h + k
                            i = mm3(bks[t][:, :], (aH[:, a, t * P:(t + 1) * P], aL[:, a, t * P:(t + 1) * P]),
                                    (hi[:, k, :], rest[:, k, :]), h == 0 and k == 0, h == 1 and k == 3)
                        if h == 1:
                            end(i, f"{name}{t}")
                    if h == 0:
                        i.then_inc(S["half_used"], 1)
                last_job[place[(kind, c)]] = f"{name}1"

            pe.wait_ge(S["rows_in"], 16 * NROWS)
            pe.wait_ge(S["const_in"], 16)
            bk = begin("cols")
            nc.tensor.transpose(bk[:, 0:NCOL], rowsA[0:NCOL, :], ident[0:NCOL, 0:NCOL])
            end(nc.tensor.transpose(bk[:, P:P + 48], rowsB[0:48, :], ident[0:48, 0:48]), "cols")
            pe.wait_ge(S["n1_tok"], 2)
            transposes("n1T", tok3)
            pe.wait_ge(S["t_rest"], 4)
            pe.wait_ge(S["lam_prod"], 1)
            bk = begin("lam")
            end(mm(bk[:, 0:2], ones, lamp, start=True, stop=True), "lam")
            for c in (3, 4, 5):
                for hh in range(2):
                    n = f"dp{c - 3}_{hh}"
                    hi, rest = wait_split("win", c, hh)
                    bk = begin(n)
                    for f in range(2):
                        fs = slice(f * P, (f + 1) * P)
                        for k in range(KT):
                            i = mm3(bk[:, f * 256:(f + 1) * 256], (hi[:, k, fs], rest[:, k, fs]),
                                    (aH[:, k, :], aL[:, k, :]), k == 0, k == KT - 1)
                    end(i, n)
                last_job[place[("win", c)]] = n
            w = need("win", 7)
            bk = begin("dadb")
            for t in range(T):
                for k in range(KT):
                    for a in (aH, aL):
                        i = mm(bk[:, t * 8:t * 8 + 8], a[:, k, t * P:(t + 1) * P].bitcast(fp32), w[:, k, 0:8],
                               start=(k == 0 and a is aH), stop=(k == KT - 1 and a is aL))
            end(i, "dadb")
            last_job[place[("win", 7)]] = "dadb"
            for c, n in ((0, "aq"), (1, "ak"), (2, "av"), (6, "dg")):
                split_product("win", c, n)
            for x in range(3):
                if x == 0:
                    ada(1)
                pe.wait_ge(S["conv_done"], x + 1)
                for t in range(T):
                    n = f"ct{x}{t}"
                    bk = begin(n)
                    for h in range(DH):
                        i = nc.tensor.transpose(bk[:, h * P:(h + 1) * P], cout[:, 4 * x + h, t * P:(t + 1) * P], ident)
                    end(i, n)
            ada(1)
            for x in range(2):
                for t in range(T):
                    pe.wait_ge(S["a_qn"], 2 * x + t + 1)
                    n = f"aT{x}{t}"
                    bk = begin(n)
                    for pr in range(4):
                        i = nc.tensor.transpose(bk[:, pr * P:(pr + 1) * P],
                                                v3(qktok, 4)[:, 2 * x + t, pr * P:(pr + 1) * P], ident)
                    end(i, n)
            for x in range(2):
                for t in range(T):
                    wait_read(pe, f"aT{x}{t}")
            pe.wait_ge(S["bias_masked"], 1)
            qk4 = aqkT.rearrange("p (x r n) -> p x r n", x=2, r=4)
            for h in range(AH):
                pb, pr = 64 * (h % 2), h // 2
                bk = begin(f"as{h}")
                mm(bk[:, 0:P], qk4[pb:pb + 64, 0, pr, 0:P], qk4[pb:pb + 64, 1, pr, 0:P], start=True, stop=False)
                mm(bk[:, 0:P], bias[:, h, 0:P], flip, start=False, stop=True)
                mm(bk[:, P:384], qk4[pb:pb + 64, 0, pr, P:256], qk4[pb:pb + 64, 1, pr, 0:256], start=True, stop=False)
                mm(bk[:, P:256], bias[:, h, P:256], flip, start=False, stop=False)
                end(mm(bk[:, 256:384], bias[:, h, 256:384], flip, start=False, stop=True), f"as{h}")
            ada(1)
            for h in range(AH):
                pe.wait_ge(S["a_exp"], h + 1)
                bk = begin(f"apT{h}")
                for j in range(3):
                    i = nc.tensor.transpose(bk[:, j * P:(j + 1) * P], aP[:, h, j * P:(j + 1) * P], ident)
                end(i, f"apT{h}")
            for h in range(AH):
                wait_read(pe, f"apT{h}")
            av3 = v3(av, 2)
            wait_read(pe, "av0")
            wait_read(pe, "av1")
            for t in range(T):
                bk = begin(f"ao{t}")
                for h in range(AH):
                    for j in range(t + 1):
                        i = mm(bk[:, h * AD:(h + 1) * AD], aPT[:, h, (t + j) * P:(t + j + 1) * P],
                               av3[:, j, h * AD:(h + 1) * AD], start=(j == 0), stop=(j == t))
                end(i, f"ao{t}")
            pe.wait_ge(S["g_ready"], 1)
            bk = begin("dec")
            mm(bk[:, 0:8], K("cumT"), gl, start=True, stop=True)
            mm(bk[:, 8:16], K("blk"), gl, start=True, stop=True)
            end(mm(bk[:, 16:32], ones, ghalf, start=True, stop=True), "dec")
            ada(1)
            pe.wait_ge(S["cumg"], 1)
            for t in range(T):
                bk = begin(f"R{t}")
                end(mm(bk[:, :], ones, YY[:, t * 512:(t + 1) * 512], start=True, stop=True), f"R{t}")
            ada(1)
            for x, src in enumerate((DK, KB, DQ, QD)):
                pe.wait_ge(S["dscaled"], x + 1)
                for t in range(T):
                    bk = begin(f"dT{x}{t}")
                    for h in range(DH):
                        o = (4 * t + h) * P
                        i = nc.tensor.transpose(bk[:, h * P:(h + 1) * P], src[:, o:o + P], ident)
                    end(i, f"dT{x}{t}")
            for x in range(3):
                for t in range(T):
                    wait_read(pe, f"dT{x}{t}")
            for x, rhs in enumerate((kbT, qT)):
                for t in range(T):
                    bk = begin(f"kk{x}{t}")
                    for h in range(DH):
                        o = (4 * t + h) * P
                        i = mm(bk[:, h * P:(h + 1) * P], kT[:, o:o + P], rhs[:, o:o + P], start=True, stop=True)
                    end(i, f"kk{x}{t}")
            ada(1)
            for t in range(T):
                pe.wait_ge(S["d_init"], t + 1)
                bk = begin(f"D0{t}")
                for h in range(DH):
                    o = (4 * t + h) * P
                    i = nc.tensor.transpose(bk[:, h * P:(h + 1) * P], DT[:, o:o + P], ident)
                end(i, f"D0{t}")
            for l, s in enumerate(LEVELS):
                last = s == LEVELS[-1]
                for t in range(T):
                    pe.wait_ge(S["am_ready"], 2 * l + t + 1)
                    wait_read(pe, f"D0{t}" if l == 0 else f"Dn{l - 1}{t}")
                    bk = begin(f"Y{l}{t}")
                    for h in range(DH):
                        o = (4 * t + h) * P
                        i = mm(bk[:, h * P:(h + 1) * P], AM[:, o:o + P], DI[:, o:o + P], start=True, stop=True)
                    end(i, f"Y{l}{t}")
                if not last:
                    ada(2 if l < 2 else 1)
                for t in range(T):
                    wait_read(pe, f"Y{l}{t}")
                    if not last:
                        bk = begin(f"Dn{l}{t}")
                        for h in range(DH):
                            o = (4 * t + h) * P
                            i = mm(bk[:, h * P:(h + 1) * P], DT[:, o:o + P], YY[:, o:o + P], start=True, stop=True)
                        end(i, f"Dn{l}{t}")
                    bk = begin(f"Dt{l}{t}")
                    for h in range(DH):
                        o = (4 * t + h) * P
                        i = mm(bk[:, h * P:(h + 1) * P], YY[:, o:o + P], DT[:, o:o + P], start=True, stop=True)
                    end(i, f"Dt{l}{t}")
                for t in range(T):
                    wait_read(pe, f"Dt{l}{t}")
            for t in range(T):
                bk = begin(f"val{t}")
                for h in range(DH):
                    o = (4 * t + h) * P
                    i = mm(bk[:, h * P:(h + 1) * P], DT[:, o:o + P], DV[:, o:o + P], start=True, stop=True)
                end(i, f"val{t}")
                bk = begin(f"kc{t}")
                for h in range(DH):
                    o = (4 * t + h) * P
                    i = mm(bk[:, h * P:(h + 1) * P], KBE[:, o:o + P], DT[:, o:o + P], start=True, stop=True)
                end(i, f"kc{t}")
            for n in range(4):
                t, r = n // 2, C * (n % 2)
                if n == 0:
                    for x in (0, 1):
                        wait_read(pe, f"kc{x}")
                        wait_read(pe, f"dT3{x}")
                else:
                    pe.wait_ge(S["s_new"], n)
                    bk = begin(f"vp{n}")
                    for h in range(DH):
                        o = (4 * t + h) * P
                        i = mm(bk[r:r + C, h * P:(h + 1) * P], KC[:, o + r:o + r + C], ST[:, h * P:(h + 1) * P],
                               start=True, stop=True)
                    end(i, f"vp{n}")
                pe.wait_ge(S["vn_new"], n + 1)
                if n < 3:
                    bk = begin(f"sn{n}")
                    for h in range(DH):
                        o = (4 * t + h) * P
                        i = mm(bk[:, h * P:(h + 1) * P], KTL[r:r + C, o:o + P], VN[r:r + C, o:o + P],
                               start=True, stop=True)
                    end(i, f"sn{n}")
                bk = begin(f"do{n}")
                for h in range(DH):
                    o = (4 * t + h) * P
                    if n:
                        mm(bk[r:r + C, h * P:(h + 1) * P], qdT[:, o + r:o + r + C], ST[:, h * P:(h + 1) * P],
                           start=True, stop=False)
                    i = mm(bk[r:r + C, h * P:(h + 1) * P], MT[r:r + C, o + r:o + r + C], VN[r:r + C, o:o + P],
                           start=(n == 0), stop=True)
                end(i, f"do{n}")
            assert adas[0] == 12
            for c in range(12):
                wait_read(pe, f"mod{c}")
            for x in range(3):
                bk = begin(f"mc{x}")
                for c in range(4):
                    i = nc.tensor.transpose(bk[:, c * P:(c + 1) * P], mrow[:, (4 * x + c) * P:(4 * x + c + 1) * P], ident)
                end(i, f"mc{x}")
            pe.wait_ge(S["o_tok"], 1)
            transposes("oT", tok3)
            wait_actT("oT")
            for c in range(2):
                tok_product("wout", c, f"mo{c}")
            pe.wait_ge(S["n2_tok"], 2)
            transposes("n2T", tok3)
            pe.wait_ge(S["t_rest"], 8)
            for c in range(8):
                for hh in range(2):
                    n = f"z{2 * c + hh}"
                    hi, rest = wait_split("ff1", c, hh)
                    bk = begin(n)
                    for f in range(2):
                        fs = slice(f * P, (f + 1) * P)
                        for k in range(KT):
                            i = mm3(bk[:, f * 256:(f + 1) * 256], (hi[:, k, fs], rest[:, k, fs]),
                                    (aH[:, k, :], aL[:, k, :]), k == 0, k == KT - 1)
                    end(i, n)
                last_job[place[("ff1", c)]] = n
            bks = [begin(f"y{j}") for j in range(4)]
            for c in range(8):
                pe.wait_ge(S["z_done"], 2 * c + 2)
                for f in range(4):
                    if f % 2 == 0:
                        hi, rest = wait_split("ff2", c, f // 2)
                    for j in range(4):
                        t, hh = j // 2, j % 2
                        ts, hs = slice(t * P, (t + 1) * P), slice(hh * 512, (hh + 1) * 512)
                        i = mm3(bks[j][:, :], (zTR[:, 4 * c + f, ts], zTLR[:, 4 * c + f, ts]),
                                (hi[:, f % 2, hs], rest[:, f % 2, hs]), c == 0 and f == 0, c == 7 and f == 3)
                        if f == 1 and j == 3:
                            i.then_inc(S["half_used"], 1)
                        if c == 7 and f == 3 and j < 3:
                            end(i, f"y{j}")
                if c < 7:
                    i.then_inc(S["ff2_used"], 1)
                else:
                    end(i, "y3")
                    last_job[place[("ff2", 7)]] = "y3"
            pe.wait_ge(S["n3_tok"], 2)
            transposes("n3T", tok3)
            pe.wait_ge(S["t_rest"], 12)
            ROPE = {0: 0, 1: 1, 6: 2, 7: 3, 8: 4, 9: 5}

            def rope_transposes(x):
                for t in range(T):
                    pe.wait_ge(S["rope_out"], 2 * x + t + 1)
                    n = f"rT{x}{t}"
                    bk = begin(n)
                    for h in range(RH):
                        i = nc.tensor.transpose(bk[:, h * P:(h + 1) * P],
                                                ropeO[:, t * 512 + h * P:t * 512 + (h + 1) * P], ident)
                    end(i, n)

            pend = []
            for c in range(16):
                split_product("win2", c, f"p{c}_")
                for x in pend:
                    rope_transposes(x)
                pend = [ROPE[c]] if c in ROPE else []
            for x in range(6):
                for t in range(T):
                    wait_read(pe, f"rT{x}{t}")
            for t in range(T):
                bk = begin(f"rs{t}")
                for h in range(RH):
                    i = mm(bk[:, h * P:(h + 1) * P], qkT2[:, 1, h, t * P:(t + 1) * P], qkT2[:, 0, h, t * P:(t + 1) * P],
                           start=True, stop=True)
                end(i, f"rs{t}")
            pe.wait_ge(S["kz_done"], 1)
            for c in (2, 3):
                for t in range(T):
                    wait_read(pe, f"p{c}_{t}")
            for hh in range(2):
                bk = begin(f"kv{hh}")
                for h in range(2):
                    hd = 2 * hh + h
                    i = mm(bk[:, h * 256:(h + 1) * 256], KZ[:, hd * P:(hd + 1) * P], RVt[:, hd * 256:(hd + 1) * 256],
                           start=True, stop=True)
                end(i, f"kv{hh}")
            for t in range(T):
                pe.wait_ge(S["st_done"], t + 1)
                for hh in range(2):
                    bk = begin(f"ro{t}{hh}")
                    for h in range(2):
                        hd = 2 * hh + h
                        i = mm(bk[:, h * 256:(h + 1) * 256], sT[:, t * 512 + hd * P:t * 512 + (hd + 1) * P],
                               RVt[:, t * 1024 + hd * 256:t * 1024 + (hd + 1) * 256], start=True, stop=True)
                    end(i, f"ro{t}{hh}")
            for hh in range(2):
                wait_read(pe, f"kv{hh}")
                bk = begin(f"rx{hh}")
                for h in range(2):
                    hd = 2 * hh + h
                    i = mm(bk[:, h * 256:(h + 1) * 256], qkT2[:, 0, hd, P:256], KV[:, hd * 256:(hd + 1) * 256],
                           start=True, stop=True)
                end(i, f"rx{hh}")
            for x in range(8):
                h, cc = x // 2, x % 2
                hq = 2 * h + cc
                q = qkT2[:, 2 + hq // 4, hq % 4, :]
                k = qkT2[:, 4 + hq // 4, hq % 4, :]
                bk = begin(f"ps{x}")
                mm(bk[:, 0:P], q[:, 0:P], k[:, 0:P], start=True, stop=False)
                mm(bk[:, 0:P], K("causT"), ident, start=False, stop=True)
                mm(bk[:, P:384], q[:, P:256], k[:, 0:256], start=True, stop=False)
                end(mm(bk[:, 256:384], K("causT"), ident, start=False, stop=True), f"ps{x}")
            pe.wait_ge(S["r_tok"], 2)
            transposes("rtT", tok3)
            wait_actT("rtT")
            for c in range(2):
                tok_product("wret", c, f"rp{c}")
            for h in range(RH):
                pe.wait_ge(S["a_done"], h + 1)
                bk = begin(f"pT{h}")
                for j in range(3):
                    i = nc.tensor.transpose(bk[:, j * P:(j + 1) * P], P2[:, 2 * h, j * P:(j + 1) * P], ident)
                end(i, f"pT{h}")
            for h in range(RH):
                wait_read(pe, f"pT{h}")
            for c in (10, 11):
                for t in range(T):
                    wait_read(pe, f"p{c}_{t}")
            for t in range(T):
                for hh in range(2):
                    bk = begin(f"po{t}{hh}")
                    for h in range(2):
                        hd = 2 * hh + h
                        for j in range(t + 1):
                            i = mm(bk[:, h * 256:(h + 1) * 256], PT2[:, hd, (t + j) * P:(t + j + 1) * P],
                                   DVt[:, j * 1024 + hd * 256:j * 1024 + (hd + 1) * 256], start=(j == 0), stop=(j == t))
                    end(i, f"po{t}{hh}")
            pe.wait_ge(S["r_tok"], 4)
            transposes("dtT", tok3)
            wait_actT("dtT")
            for c in range(2):
                tok_product("wdiff", c, f"wd{c}")
            pe.wait_ge(S["diag"], 1)
            for x in range(4):
                bk = begin(f"gr{x}")
                end(mm(bk[:, :], ones, gdiag[:, x * 512:(x + 1) * 512], start=True, stop=True), f"gr{x}")
            pe.wait_ge(S["m_done"], 1)
            transposes("mT", v3(GR, 2))
            wait_actT("mT")
            for c in range(2):
                tok_product("wout2", c, f"xo{c}")
            pe.wait_ge(S["n4_tok"], 2)
            transposes("n4T", tok3)
            wait_actT("n4T")
            pe.wait_ge(S["wr_in"], 32)
            bk = begin("rout")
            for t in range(T):
                for k in range(KT):
                    i = mm(bk[:, t * 36:t * 36 + 36], aT[:, k, t * P:(t + 1) * P], wr[:, k, :],
                           start=(k == 0), stop=(k == KT - 1))
            end(i, "rout")
            for t in range(T):
                for hh in range(2):
                    bk = begin(f"hb{t}{hh}")
                    for k in range(4):
                        i = nc.tensor.transpose(bk[:, k * P:(k + 1) * P], aT[:, 4 * hh + k, t * P:(t + 1) * P], ident)
                    end(i, f"hb{t}{hh}")
            pe.wait_ge(S["sel_ready"], 1)
            bk = begin("rank")
            mm(bk[:, 0:32], K("before"), sel[:, 0:32], start=True, stop=True)
            mm(bk[:, 32:64], ones, sel[:, 0:32], start=True, stop=False)
            mm(bk[:, 32:64], K("before"), sel[:, 32:64], start=False, stop=True)
            mm(bk[:, 64:96], ones, sel[:, 0:32], start=True, stop=False)
            end(mm(bk[:, 64:96], ones, sel[:, 32:64], start=False, stop=True), "rank")
            base[:] = uses
            for b in range(8):
                pe.wait_ge(read[b], base[b])
            for t in range(T):
                for hh in range(2):
                    wait_read(pe, f"hb{t}{hh}")
            pe.wait_ge(S["moe_zero"], 1)

            def gather():
                for k in range(KT):
                    for t in range(T):
                        i = mm(banks[BX][:, k * SL:(k + 1) * SL], tok3[:, t, k * P:(k + 1) * P],
                               Pm[:, t * SL:(t + 1) * SL], start=(t == 0), stop=(t == 1))
                return i

            def gate_up(wg, wu):
                for m, w in ((0, wg), (1, wu)):
                    for k in range(KT):
                        for hf in range(2):
                            i = mm(banks[BG][hf * SL:(hf + 1) * SL, m * 256:(m + 1) * 256], xg[:, k * SL:(k + 1) * SL],
                                   w[:, k, hf * 256:(hf + 1) * 256], start=(k == 0), stop=(k == KT - 1))
                return i

            def turn(pw):
                for j in range(2):
                    nc.tensor.transpose(banks[BH][:, j * P:(j + 1) * P], hid[:, j * P:(j + 1) * P], ident)
                for t in range(T):
                    i = nc.tensor.transpose(banks[BH][:, 256 + t * P:256 + (t + 1) * P], pw[:, t * P:(t + 1) * P], ident)
                return i

            def down(wd):
                for f in range(4):
                    o = (f % 2) * P + (f // 2) * SL
                    for hf in range(2):
                        i = mm(banks[BO][hf * SL:(hf + 1) * SL, :], hidT[:, o:o + SL], wd[:, f, hf * 512:(hf + 1) * 512],
                               start=(f == 0), stop=(f == 3))
                return i

            def scatter(pt, start=False, stop=False):
                for j in range(4):
                    t, hh = j // 2, j % 2
                    i = mm(banks[4 + j][:, :], pt[hh][:, t * P:(t + 1) * P], ysb, start=start, stop=stop,
                           skip_group_check=True)
                return i

            scatter(PT[1], start=True)
            pe.wait_ge(S["p_ready"], 1)
            gather().then_inc(full[BX], 1)
            with pe.Fori(0, E // 2) as it:
                for u in range(2):
                    e = 2 * it + u
                    pe.wait_ge(*moe_in(3 * u, it))
                    pe.wait_ge(*moe_in(3 * u + 1, it))
                    pe.wait_ge(read[BX], base[BX] + 2 * it + (u + 1))
                    pe.wait_ge(S["moe_hid"], 2 * it + (u + 1))
                    gate_up(v3(mslot(3 * u), KT), v3(mslot(3 * u + 1), KT)).then_inc(full[BG], 1)
                    pe.wait_ge(S["p_ready"], 2 * it + (u + 2))
                    gather().then_inc(full[BX], 1)
                    pe.wait_ge(S["moe_hid"], 2 * it + (u + 2))
                    pe.wait_ge(read[BO], base[BO] + 2 * it + u)
                    pe.wait_ge(read[BH], base[BH] + 2 * it + u)
                    turn(PwD[u]).then_inc(full[BH], 1)
                    scatter(PT[1 - u])
                    pe.wait_ge(*moe_in(3 * u + 2, it))
                    pe.wait_ge(read[BH], base[BH] + 2 * it + (u + 1))
                    down(v3(mslot(3 * u + 2), 4)).then_inc(full[BO], 1)
            pe.wait_ge(read[BO], base[BO] + E)
            scatter(PT[1]).then_inc(S["over_go"], 1)
            pe.wait_ge(S["flag_ready"], 1)
            over = pe.value_load(flagi[0:1, 0:1], min_val=0, max_val=1)
            with pe.If(over > 0):
                with pe.Fori(0, E) as e:
                    pe.wait_ge(S["over_w"], 48 * e + 48)
                    for k in range(NOVER):
                        n = NOVER * e + (k + 1)
                        pe.wait_ge(S["over_p"], n)
                        gather().then_inc(S["over_x"], 1)
                        pe.wait_ge(S["over_xg"], n)
                        gate_up(v3(mslot(0), KT), v3(mslot(1), KT)).then_inc(S["over_g"], 1)
                        pe.wait_ge(S["over_a"], n)
                        turn(PwD[0]).then_inc(S["over_t"], 1)
                        pe.wait_ge(S["over_te"], n)
                        down(v3(mslot(2), 4)).then_inc(S["over_d"], 1)
                        pe.wait_ge(S["over_y"], n)
                        i = scatter(PT[0])
                        i.then_inc(S["over_sc"], 1)
            pe.wait_ge(S["flag_ready"], 1)
            scatter(ZT, stop=True).then_inc(S["y_sum"], 1)

        steps = {"dve_step": 0, "act_step": 0, "pool_step": 0}

        def chain(eng, ins, name):
            steps[name] += 1
            ins.then_inc(S[name], 1)
            eng.wait_ge(S[name], steps[name])

        GAIN = {"n1T": lambda k: (col("mix", k), None),
                "oT": lambda k: (col("attout", k) if k < 4 else col("dnout"), None),
                "n2T": lambda k: (col("ffn", k), None),
                "n3T": lambda k: (sc1[:, k:k + 1], modc[:, k:k + 1]),
                "rtT": lambda k: (None, None),
                "dtT": lambda k: (dng[:, k % 2:k % 2 + 1], None),
                "mT": lambda k: (None, None),
                "n4T": lambda k: (sc2[:, k:k + 1], modc[:, 24 + k:25 + k])}

        @block.scalar
        def _(act):
            A = nc.scalar.activation

            def step(ins):
                chain(act, ins, "act_step")

            def copy(o, i):
                return A(o, i, ACT.Copy)

            def rows(name, src, i=0):
                r = colat[name] + i
                act.dma_start(rowsA[r:r + src.shape[0], 0:src.shape[1]], src).then_inc(S["rows_in"], 16)

            act.dma_start(con[:, :], g["const"]).then_inc(S["const_in"], 16)
            for name, key in (("c", "c_2"), ("mix", "mix_norm_gain"), ("attout", "att_out_gain"),
                              ("dnout", "dn_out_gain"), ("ffn", "ffn_norm_gain"), ("nmix", "norm_mix_2"),
                              ("nffn", "norm_ffn_2"), ("dnorm", "diff_norm_2"), ("bada", "b_ada_2")):
                rows(name, g[key].rearrange("o (k p) -> (o k) p", p=P))
            for name, key in (("qg", "att_q_gain"), ("kg", "att_k_gain")):
                for hh in range(2):
                    r = colat[name]
                    act.dma_start(rowsA[r:r + 1, hh * AD:(hh + 1) * AD], g[key]).then_inc(S["rows_in"], 16)
            for i, key in enumerate(("lam_q1_2", "lam_k1_2", "lam_q2_2", "lam_k2_2")):
                rows("lam", g[key], i)
            act.dma_start(rowsB[0:48, :], g["dn_conv_w"].rearrange("o j (f p) -> (o j f) p", p=P)).then_inc(S["rows_in"], 16)

            def inv_rms(o, i, n, width):
                step(A(lnv[:, 0:n], i, ACT.Ln, scale=1.0 / width, bias=EPSC))
                return A(o, lnv[:, 0:n], ACT.Exp, scale=-0.5)

            def norm(name, sem=None, counts=()):
                for t in range(T):
                    if sem:
                        act.wait_ge(S[sem], counts[t])
                    step(A(tok3[:, t, :], X3[:, t, :], ACT.Square, accum_out=ss[:, t:t + 1]))
                inv_rms(rstd, ss, T, D).then_inc(S[f"{name}_rs"], 1)

            def evac_T(name):
                for j in (0, 2):
                    bk = wait_full(act, f"{name}{j}")
                    for k in range(2):
                        sc, bi = GAIN[name](2 * j + k)
                        o = aT[:, 2 * j + k, :]
                        p = bk[:, k * 256:(k + 1) * 256]
                        if sc is None:
                            i = copy(o, p)
                        elif bi is None:
                            i = A(o, p, ACT.Copy, scale=sc)
                        else:
                            i = A(o, p, ACT.Identity, scale=sc, bias=bi)
                    done(i, f"{name}{j}")
                    if name in SPLIT_T:
                        wait_full(act, f"{name}3")
                        wait_read(act, f"{name}{j}")
                        t_high(j)
                if name in SPLIT_T:
                    for j in (1, 3):
                        wait_read(act, f"{name}{j}")
                        t_high(j)

            def t_high(j):
                A(aH[:, 2 * j:2 * j + 2, :], aT[:, 2 * j:2 * j + 2, :], ACT.Copy).then_inc(S["t_high"], 1)

            def w_high(i):
                kind, c, h = halves[i]
                n = place[(kind, c)]
                if h == 0:
                    act.wait_ge(w_in[n % NR], 16 * (n // NR + 1))
                if i >= NH:
                    wait_used(act, i - NH)
                w, hi = half(i)
                A(hi, w, ACT.Copy).then_inc(S["w_high"], 1)

            act.wait_ge(S["x_in"], 32)
            act.wait_ge(S["eps_set"], 1)
            norm("n1")
            w_high(0)
            w_high(1)
            act.wait_ge(S["ang_ready"], 1)
            A(cosin[:, :], angle[:, :], ACT.Sin).then_inc(S["ang_done"], 1)
            bk = wait_full(act, "cols")
            copy(colA[:, 0:NCOL], bk[:, 0:NCOL])
            done(copy(colB[:, :], bk[:, P:P + 48]), "cols")
            act.wait_ge(S["vec_in"], 64)
            wait_read(act, "cols")
            step(A(ea, alog, ACT.Exp))
            A(cex, col("c", 0, 8), ACT.Exp, scale=-1.0).then_inc(S["c_exp"], 1)
            evac_T("n1T")
            w_high(2)
            bk = wait_full(act, "lam")
            done(A(lame, bk[:, 0:2], ACT.Exp), "lam")
            for x in range(3):
                for hh in range(2):
                    n = f"dp{x}_{hh}"
                    w_high(2 * x + hh + NH)
                    bk = wait_full(act, n)
                    done(copy(cin[:, 4 * x + 2 * hh:4 * x + 2 * hh + 2, 3:CW], v3(bk[:, :], 2)), n)
                act.wait_ge(S["conv_y"], x + 1)
                A(cexp, cout[:, 4 * x:4 * x + 4, :], ACT.Sigmoid).then_inc(S["conv_e"], 1)
            act.wait_ge(S["gl_req"], 1)
            step(A(t3, t2, ACT.Exp, scale=-1.0))
            step(A(t3, t3, ACT.Ln, bias=ones[:, 0:1]))
            A(v3(beta, 2), v3(dadb, 2)[:, :, 4:8], ACT.Exp, scale=-1.0).then_inc(S["gl_exp"], 1)
            mods = [0]

            def mod_row(n):
                for _ in range(n):
                    c = mods[0]
                    mods[0] += 1
                    bk = wait_full(act, f"mod{c}")
                    done(copy(mrow[:, c * P:(c + 1) * P], bk[:, 0:P]), f"mod{c}")

            w_high(9)
            for x, n in enumerate(("aq", "ak")):
                if x:
                    w_high(10)
                    w_high(11)
                for t in range(T):
                    bk = wait_full(act, f"{n}{t}")
                    done(copy(v3(qktok, 4)[:, 2 * x + t, :], bk[:, :]), f"{n}{t}")
            w_high(12)
            w_high(13)
            for t in range(T):
                bk = wait_full(act, f"av{t}")
                done(copy(av[:, t * 512:(t + 1) * 512], bk[:, :]), f"av{t}")
            act.wait_ge(S["a_ss"], 4)
            step(A(a_rs, a_ss, ACT.Ln, scale=1.0 / AD, bias=EPSC))
            A(a_rs, a_rs, ACT.Exp, scale=-0.5).then_inc(S["a_rs"], 1)
            for t in range(T):
                bk = wait_full(act, f"dg{t}")
                step(copy(gate[:, t * 512:(t + 1) * 512], bk[:, :]))
                done(A(gexp[:, t * 512:(t + 1) * 512], bk[:, :], ACT.Sigmoid), f"dg{t}")
            for x, dst in enumerate((DQ, DK, DV)):
                if x == 0:
                    mod_row(1)
                for t in range(T):
                    bk = wait_full(act, f"ct{x}{t}")
                    done(copy(dst[:, t * 512:(t + 1) * 512], bk[:, :]), f"ct{x}{t}")
            mod_row(1)
            for t in range(T):
                bk = wait_full(act, f"aT0{t}")
                done(A(v3(aqkT[:, 0:1024], 4)[:, :, t * P:(t + 1) * P], v3(bk[:, :], 4), ACT.Copy, scale=qg8), f"aT0{t}")
            for h in range(AH):
                act.wait_ge(S["a_max"], h + 1)
                bk = wait_full(act, f"as{h}")
                step(A(aP[:, h, 0:P], bk[:, 0:P], ACT.Exp, bias=a_mx[:, 2 * h:2 * h + 1],
                       accum_out=a_sum[:, 2 * h:2 * h + 1]))
                step(A(aP[:, h, P:384], bk[:, P:384], ACT.Exp, bias=a_mx[:, 2 * h + 1:2 * h + 2],
                       accum_out=a_sum[:, 2 * h + 1:2 * h + 2]))
                act.sem_inc(S["a_exp"], 1)
                act.sem_inc(read[where[f"as{h}"][0]], 1)
            mod_row(1)
            for h in range(0, AH, 2):
                bk = wait_full(act, f"apT{h}")
                done(copy(aPT[:, h, :], bk[:, 0:384]), f"apT{h}")
            act.wait_ge(S["dn_ss"], 1)
            inv_rms(n_rs, n_ss, 16, 1).then_inc(S["dn_rs"], 1)
            act.wait_ge(S["dec_ready"], 1)
            step(A(edec, dec[:, 0:8], ACT.Exp))
            step(A(ecd, dec[:, 16:32], ACT.Exp))
            A(etl, t1, ACT.Exp).then_inc(S["dec_exp"], 1)
            mod_row(1)
            for t in range(T):
                act.wait_ge(S["et_req"], t + 1)
                A(ET[:, t * 512:(t + 1) * 512], ET[:, t * 512:(t + 1) * 512], ACT.Exp).then_inc(S["et_exp"], 1)
            mod_row(1)
            for x, dst in enumerate((kT, kbT, qT, qdT)):
                for t in range(T):
                    bk = wait_full(act, f"dT{x}{t}")
                    done(copy(dst[:, t * 512:(t + 1) * 512], bk[:, :]), f"dT{x}{t}")
            mod_row(1)
            for t in range(T):
                bk = wait_full(act, f"D0{t}")
                done(copy(DI[:, t * 512:(t + 1) * 512], bk[:, :]), f"D0{t}")
            for l in range(len(LEVELS)):
                for t in range(T):
                    bk = wait_full(act, f"Y{l}{t}")
                    done(copy(YY[:, t * 512:(t + 1) * 512], bk[:, :]), f"Y{l}{t}")
                if l < len(LEVELS) - 1:
                    mod_row(2 if l < 2 else 1)
            for t in range(T):
                bk = wait_full(act, f"val{t}")
                done(copy(VAL[:, t * 512:(t + 1) * 512], bk[:, :]), f"val{t}")
                bk = wait_full(act, f"kc{t}")
                done(copy(KC[:, t * 512:(t + 1) * 512], bk[:, :]), f"kc{t}")
            for n in range(4):
                t, r = n // 2, C * (n % 2)
                bk = wait_full(act, f"do{n}")
                done(copy(odn[r:r + C, t * 512:(t + 1) * 512], bk[r:r + C, :]), f"do{n}")
            act.wait_ge(S["o_ss"], 2)
            step(A(lnv[:, 0:8], n_ss[:, 0:8], ACT.Ln, scale=1.0 / DD, bias=EPSC))
            step(A(n_rs[:, 0:8], lnv[:, 0:8], ACT.Exp, scale=-0.5))
            inv_rms(rstd, ss, T, 512).then_inc(S["o_rs"], 1)
            evac_T("oT")
            for i in range(F1, F1 + NH):
                w_high(i)
            norm("n2", "x1_new", (3, 4))
            evac_T("n2T")
            for c in range(16):
                bk = wait_full(act, f"z{c}")
                if c >= 2:
                    act.wait_ge(S["z_done"], c - 1)
                w_high(F1 + c + NH)
                done(A(zr[:, (c % 2) * 512:(c % 2 + 1) * 512], bk[:, :], ACT.Relu), f"z{c}")
            for i in range(F1 + 16 + NH, W2 + 2):
                w_high(i)
            norm("n3", "x2_new", (2, 4))
            evac_T("n3T")
            w_high(W2 + 2)
            def rope_evac(x):
                for t in range(T):
                    bk = wait_full(act, f"rT{x}{t}")
                    done(copy(qkT2[:, x, :, t * P:(t + 1) * P], v3(bk[:, :], 4)), f"rT{x}{t}")

            ROPE = {0: 0, 1: 1, 6: 2, 7: 3, 8: 4, 9: 5}
            pend = []
            for c in range(16):
                if 2 * c + 3 < 32:
                    w_high(W2 + 2 * c + 3)
                for t in range(T):
                    n = f"p{c}_{t}"
                    o = t * 1024 + (c % 2) * 512
                    if c in (2, 3, 10, 11):
                        bk = wait_full(act, n)
                        done(copy((RVt if c < 4 else DVt)[:, o:o + 512], bk[:, :]), n)
                    elif c in (4, 5):
                        bk = wait_full(act, n)
                        step(copy(RG[:, o:o + 512], bk[:, :]))
                        i = 2 * (c - 4) + t
                        if i >= 2:
                            act.wait_ge(S["gate2"], i - 1)
                        A(gex[:, t * 512:(t + 1) * 512], bk[:, :], ACT.Sigmoid).then_inc(S["g_exp"], 1)
                        act.wait_ge(S["g_exp"], i + 1)
                        act.sem_inc(read[where[n][0]], 1)
                    elif c >= 12:
                        bk = wait_full(act, n)
                        done(A((GR if c < 14 else GD)[:, o:o + 512], bk[:, :], ACT.Sigmoid), n)
                if 2 * c + 4 < 32:
                    w_high(W2 + 2 * c + 4)
                for x in pend:
                    rope_evac(x)
                pend = [ROPE[c]] if c in ROPE else []
            for hh in range(2):
                bk = wait_full(act, f"kv{hh}")
                done(copy(KV[:, hh * 512:(hh + 1) * 512], bk[:, :]), f"kv{hh}")
            for t in range(T):
                for hh in range(2):
                    bk = wait_full(act, f"ro{t}{hh}")
                    done(copy(tok[:, t * 1024 + hh * 512:t * 1024 + (hh + 1) * 512], bk[:, :]), f"ro{t}{hh}")
            act.wait_ge(S["head_ss"], 1)
            inv_rms(n_rs[:, 0:8], n_ss[:, 0:8], 8, RV).then_inc(S["head_rs"], 1)
            for x in range(8):
                act.wait_ge(S["p_max"], x + 1)
                bk = wait_full(act, f"ps{x}")
                step(A(P2[:, x, 0:P], bk[:, 0:P], ACT.Exp, scale=RK ** -0.5, bias=a_mx[:, 2 * x:2 * x + 1],
                       accum_out=a_sum[:, 2 * x:2 * x + 1]))
                step(A(P2[:, x, P:384], bk[:, P:384], ACT.Exp, scale=RK ** -0.5, bias=a_mx[:, 2 * x + 1:2 * x + 2],
                       accum_out=a_sum[:, 2 * x + 1:2 * x + 2]))
                act.sem_inc(S["p_exp"], 1)
                act.sem_inc(read[where[f"ps{x}"][0]], 1)
            evac_T("rtT")
            for h in range(0, RH, 2):
                bk = wait_full(act, f"pT{h}")
                done(copy(PT2[:, h, :], bk[:, 0:384]), f"pT{h}")
            for t in range(T):
                for hh in range(2):
                    bk = wait_full(act, f"po{t}{hh}")
                    done(copy(tok[:, t * 1024 + hh * 512:t * 1024 + (hh + 1) * 512], bk[:, :]), f"po{t}{hh}")
            act.wait_ge(S["head_ss"], 2)
            inv_rms(n_rs[:, 0:8], n_ss[:, 0:8], 8, RV).then_inc(S["head_rs"], 1)
            evac_T("dtT")
            for x in range(4):
                bk = wait_full(act, f"gr{x}")
                done(copy((grow1 if x < 2 else grow2)[:, (x % 2) * 512:(x % 2 + 1) * 512], bk[:, :]), f"gr{x}")
            evac_T("mT")
            norm("n4", "x3_new", (3, 4))
            evac_T("n4T")
            act.wait_ge(S["router_req"], 1)
            A(rt[:, 0:8], rt[:, 0:8], ACT.Exp).then_inc(S["router_exp"], 1)
            act.wait_ge(S["router_req"], 2)
            A(rs8[:, 8:10], rs8[:, 8:10], ACT.Exp).then_inc(S["router_exp"], 1)
            for t in range(T):
                for hh in range(2):
                    bk = wait_full(act, f"hb{t}{hh}")
                    done(copy(tok3[:, t, hh * 512:(hh + 1) * 512], bk[:, :]), f"hb{t}{hh}")
            act.wait_ge(S["moe_zero"], 1)

            def out_turned(pt):
                copy(hidT, banks[BH][:, 0:256])
                copy(pt[0][0:SL, :], banks[BH][0:SL, 256:512])
                return copy(pt[1][SL:P, :], banks[BH][SL:P, 256:512])

            act.wait_ge(full[BX], base[BX] + 1)
            copy(xg, banks[BX][:, :]).then_inc(read[BX], 1)
            with act.Fori(0, E // 2) as it:
                for u in range(2):
                    act.wait_ge(full[BG], base[BG] + 2 * it + (u + 1))
                    act.wait_ge(S["moe_hid"], 2 * it + (u + 1))
                    A(gex2, banks[BG][:, 0:256], ACT.Sigmoid).then_inc(S["moe_exp"], 1)
                    act.wait_ge(full[BX], base[BX] + 2 * it + (u + 2))
                    copy(xg, banks[BX][:, :]).then_inc(read[BX], 1)
                    act.wait_ge(full[BH], base[BH] + 2 * it + (u + 1))
                    act.wait_ge(full[BO], base[BO] + 2 * it + u)
                    out_turned(PT[u]).then_inc(read[BH], 1)
                    act.wait_ge(full[BO], base[BO] + 2 * it + (u + 1))
                    copy(ysb, banks[BO][:, :]).then_inc(read[BO], 1)
            act.wait_ge(S["flag_ready"], 1)
            over = act.value_load(flagi[0:1, 0:1], min_val=0, max_val=1)
            with act.If(over > 0):
                with act.Fori(0, E) as e:
                    for k in range(NOVER):
                        n = NOVER * e + (k + 1)
                        act.wait_ge(S["over_x"], n)
                        copy(xg, banks[BX][:, :]).then_inc(S["over_xg"], 1)
                        act.wait_ge(S["over_g"], n)
                        A(gex2, banks[BG][:, 0:256], ACT.Sigmoid).then_inc(S["over_e"], 1)
                        act.wait_ge(S["over_t"], n)
                        out_turned(PT[0]).then_inc(S["over_te"], 1)
                        act.wait_ge(S["over_d"], n)
                        copy(ysb, banks[BO][:, :]).then_inc(S["over_y"], 1)
            act.wait_ge(S["y_done"], 1)
            norm("n5")
            act.wait_ge(S["out_done"], 1)
            for t in range(T):
                act.dma_start(out[0, t * P:(t + 1) * P, :], tok3[:, t, :]).then_inc(S["store"], 16)
            act.wait_ge(S["store"], 16 * T)

        @block.vector
        def _(dve):
            V = nc.vector
            TS, TT, STT = V.tensor_scalar, V.tensor_tensor, V.scalar_tensor_tensor

            def step(ins):
                chain(dve, ins, "dve_step")

            def tt(o, a, b, op):
                step(TT(o, a, b, op))

            def norm_tok(name):
                dve.wait_ge(S[f"{name}_rs"], 1)
                for t in range(T):
                    TS(tok3[:, t, :], X3[:, t, :], rstd[:, t:t + 1], None, ALU.mult).then_inc(S[f"{name}_tok"], 1)

            def evac_T(name):
                for j in (1, 3):
                    bk = wait_full(dve, f"{name}{j}")
                    for k in range(2):
                        sc, bi = GAIN[name](2 * j + k)
                        o = aT[:, 2 * j + k, :]
                        p = bk[:, k * 256:(k + 1) * 256]
                        if sc is None:
                            i = V.tensor_copy(o, p)
                        elif bi is None:
                            i = TS(o, p, sc, None, ALU.mult)
                        else:
                            i = TS(o, p, sc, bi, ALU.mult, ALU.add)
                    done(i, f"{name}{j}")
                if name in SPLIT_T:
                    for n, j in enumerate((0, 2, 1, 3)):
                        dve.wait_ge(S["t_high"], 4 * SPLIT_T[name] + n + 1)
                        js = slice(2 * j, 2 * j + 2)
                        TT(aL[:, js, :], aT[:, js, :], aH[:, js, :].bitcast(fp32), ALU.subtract).then_inc(S["t_rest"], 1)

            def w_rest(i):
                dve.wait_ge(S["w_high"], i + 1)
                w, hi = half(i)
                TT(half(i, ringR)[0], w, hi.bitcast(fp32), ALU.subtract).then_inc(S["w_rest"], 1)

            V.memset(EPSC, EPS).then_inc(S["eps_set"], 1)
            dve.wait_ge(S["pos_in"], 16)
            dve.wait_ge(S["const_in"], 16)
            step(V.tensor_copy(posf, posi[:, :]))
            a4, k4 = v3(angle[:, :], 4), v3(angk[:, :], 4)
            for x in range(4):
                step(TS(a4[:, x, :], K("inv"), posf[:, x % 2:x % 2 + 1], None, ALU.mult))
            step(TS(angk[:, 0:128], angle[:, 0:128], 1 / (2 * np.pi), 0.25, ALU.mult, ALU.add))
            step(TS(angk[:, 128:256], angle[:, 128:256], 1 / (2 * np.pi), None, ALU.mult))
            step(TS(angk[:, :], angk[:, :], 12582912.0, None, ALU.add))
            step(TS(angk[:, :], angk[:, :], -12582912.0, None, ALU.add))
            for cw in (6.28125, 0.0019350051879882812, 3.0199159819e-7):
                step(STT(angle[:, :], angk[:, :], -cw, angle[:, :], ALU.mult, ALU.add))
            step(TS(angle[:, 0:128], angle[:, 0:128], float(np.pi / 2), None, ALU.add))
            TS(angle[:, :], angle[:, :], 3.1415925, -3.1415925, ALU.min, ALU.max).then_inc(S["ang_ready"], 1)
            norm_tok("n1")
            w_rest(0)
            w_rest(1)
            wait_read(dve, "cols")
            evac_T("n1T")
            w_rest(2)
            step(TS(qg8, col("qg"), AD ** -0.5, None, ALU.mult))
            step(TS(dng, col("dnorm", 0, 2), 1.0 - LAMI, None, ALU.mult))
            l2 = colA[:, colat["lam"]:colat["lam"] + 4].rearrange("p (a b) -> p b a", b=2)
            TT(lamp, l2[:, 0, :], l2[:, 1, :], ALU.mult).then_inc(S["lam_prod"], 1)
            dve.wait_ge(S["c_exp"], 1)
            step(TS(cex, cex, 1.0, None, ALU.add))
            step(V.reciprocal(cex, cex))
            step(TT(cs, cex, col("c", 0, 8), ALU.mult))
            dve.wait_ge(S["cin_zero"], 1)
            for x in range(3):
                for f in range(4 * x, 4 * x + 4):
                    if f % 2 == 0:
                        w_rest(f // 2 + NH)
                        wait_read(dve, f"dp{x}_{(f % 4) // 2}")
                    step(TS(cout[:, f, :], cin[:, f, 0:256], colB[:, f:f + 1], None, ALU.mult))
                    for j in range(1, 4):
                        i = STT(cout[:, f, :], cin[:, f, j:j + 256], colB[:, j * 12 + f:j * 12 + f + 1],
                                cout[:, f, :], ALU.mult, ALU.add)
                        if f % 4 < 3 or j < 3:
                            step(i)
                i.then_inc(S["conv_y"], 1)
                dve.wait_ge(S["conv_e"], x + 1)
                TT(cout[:, 4 * x:4 * x + 4, :], cout[:, 4 * x:4 * x + 4, :], v3(cexp, 4), ALU.mult)\
                    .then_inc(S["conv_done"], 1)
                dve.wait_ge(S["conv_done"], x + 1)
            bk = wait_full(dve, "dadb")
            done(V.tensor_copy(dadb, bk[:, 0:16]), "dadb")
            wait_read(dve, "dadb")
            tt(v3(t1, 2), v3(dadb, 2)[:, :, 0:4], bm(dtb, 2), ALU.add)
            STT(t2, t1, -1.0, t1, ALU.mult, ALU.max).then_inc(S["gl_req"], 1)
            dve.wait_ge(S["gl_exp"], 1)
            step(STT(gl, t1, 0.0, t3, ALU.max, ALU.add))
            tt(v3(gl, 2), v3(gl, 2), bm(ea, 2), ALU.mult)
            step(TS(beta, beta, 1.0, None, ALU.add))
            step(V.reciprocal(beta, beta))
            step(TS(gl, gl, -1.0, None, ALU.mult))
            TT(v3(ghalf, 2), bm(gl, 2), bc(K("half"), 8), ALU.mult).then_inc(S["g_ready"], 1)
            w_rest(9)
            for x in range(2):
                if x:
                    w_rest(10)
                    w_rest(11)
                for t in range(T):
                    wait_read(dve, f"{'ak' if x else 'aq'}{t}")
                    q = v3(qktok, 4)[:, 2 * x + t, :]
                    s = v3(asq, 4)[:, 2 * x + t, :]
                    tt(s, q, q, ALU.mult)
                    o = (2 * x + t) * AH
                    V.tensor_reduce(a_ss[:, o:o + AH], v3(s, AH), AX.X, ALU.add).then_inc(S["a_ss"], 1)
            w_rest(12)
            w_rest(13)
            dve.wait_ge(S["a_rs"], 1)
            for xt in range(4):
                q = v3(v3(qktok, 4)[:, xt, :], AH)
                TT(q, q, bc(a_rs[:, xt * AH:(xt + 1) * AH], AD), ALU.mult).then_inc(S["a_qn"], 1)
            wait_full(dve, "dg1")
            V.tensor_copy(v3(csb, KT), bc(cs, 32)).then_inc(S["c_silu"], 1)
            for t in range(T):
                wait_read(dve, f"dg{t}")
            tt(gate, gate, gexp, ALU.mult)
            for t in range(T):
                bk = wait_full(dve, f"aT1{t}")
                done(TS(v3(aqkT[:, 1024:2048], 4)[:, :, t * P:(t + 1) * P], v3(bk[:, :], 4), col("kg"), None, ALU.mult), f"aT1{t}")
            for h in range(AH):
                bk = wait_full(dve, f"as{h}")
                step(V.tensor_reduce(a_mx[:, 2 * h:2 * h + 1], bk[:, 0:P], AX.X, ALU.max, negate=True))
                V.tensor_reduce(a_mx[:, 2 * h + 1:2 * h + 2], bk[:, P:384], AX.X, ALU.max, negate=True)\
                    .then_inc(S["a_max"], 1)
            dve.wait_ge(S["a_exp"], AH)
            for h in range(1, AH, 2):
                bk = wait_full(dve, f"apT{h}")
                done(V.tensor_copy(aPT[:, h, :], bk[:, 0:384]), f"apT{h}")
            step(V.reciprocal(a_rd, a_sum))
            for t in range(T):
                bk = wait_full(dve, f"ao{t}")
                done(TT(v3(oatt[:, t * 512:(t + 1) * 512], AH), v3(bk[:, :], AH),
                        bc(a_rd.rearrange("p (h t) -> p t h", t=2)[:, t, :], AD), ALU.mult), f"ao{t}")
                wait_read(dve, f"ao{t}")
            for x, src in enumerate((DQ, DK)):
                for t in range(T):
                    wait_read(dve, f"ct{x}{t}")
                tt(dsq, src, src, ALU.mult)
                i = V.tensor_reduce(n_ss[:, 8 * x:8 * x + 8], v3(dsq, 8), AX.X, ALU.add)
                if x == 0:
                    step(i)
            i.then_inc(S["dn_ss"], 1)
            TT(v3(YY, 8), bm(K("cumT"), 8), bc(gl, P), ALU.mult).then_inc(S["cumg"], 1)
            bk = wait_full(dve, "dec")
            done(V.tensor_copy(dec, bk[:, 0:32]), "dec")
            wait_read(dve, "dec")
            TT(t1, dec[:, 8:16], dec[:, 0:8], ALU.subtract).then_inc(S["dec_ready"], 1)
            for t in range(T):
                bk = wait_full(dve, f"R{t}")
                e = v3(ET[:, t * 512:(t + 1) * 512], 4)
                done(TT(e, v3(bk[:, :], 4), bc(dec[:, 4 * t:4 * t + 4], P), ALU.subtract), f"R{t}")
                wait_read(dve, f"R{t}")
                TT(e, e, bm(K("negT"), 4), ALU.add).then_inc(S["et_req"], 1)
            dve.wait_ge(S["dn_rs"], 1)
            step(TS(n_rs[:, 0:8], n_rs[:, 0:8], DD ** -0.5, None, ALU.mult))
            TT(v3(DK, 8), v3(DK, 8), bc(n_rs[:, 8:16], P), ALU.mult).then_inc(S["dscaled"], 1)
            dve.wait_ge(S["dscaled"], 1)
            TT(v3(KB, 8), v3(DK, 8), bc(beta, P), ALU.mult).then_inc(S["dscaled"], 1)
            TT(v3(DQ, 8), v3(DQ, 8), bc(n_rs[:, 0:8], P), ALU.mult).then_inc(S["dscaled"], 1)
            dve.wait_ge(S["dec_exp"], 1)
            dve.wait_ge(S["dscaled"], 3)
            TT(v3(QD, 8), v3(DQ, 8), bc(edec, P), ALU.mult).then_inc(S["dscaled"], 1)
            tt(v3(KBE, 8), v3(KB, 8), bc(edec, P), ALU.mult)
            tt(v3(KTL, 8), v3(DK, 8), bc(etl, P), ALU.mult)
            for t in range(T):
                wait_read(dve, f"ct2{t}")
            tt(v3(DV, 8), v3(DV, 8), bc(beta, P), ALU.mult)
            for x, dst in enumerate((AT, MT)):
                for t in range(T):
                    dve.wait_ge(S["et_exp"], t + 1)
                    bk = wait_full(dve, f"kk{x}{t}")
                    o = slice(t * 512, (t + 1) * 512)
                    done(TT(dst[:, o], bk[:, :], ET[:, o], ALU.mult), f"kk{x}{t}")
                    wait_read(dve, f"kk{x}{t}")
                    if x == 0:
                        tt(v3(DT[:, o], 4), v3(AT[:, o], 4), bm(K("lvl1"), 4), ALU.mult)
                        TT(v3(DT[:, o], 4), v3(DT[:, o], 4), bm(ident, 4), ALU.add).then_inc(S["d_init"], 1)
            for l, s in enumerate(LEVELS):
                for t in range(T):
                    o = slice(t * 512, (t + 1) * 512)
                    if s != LEVELS[-1]:
                        bk = wait_full(dve, f"Dn{l}{t}")
                        wait_full(dve, f"Dt{l}{t}")
                        done(TT(DI[:, o], bk[:, :], DI[:, o], ALU.add), f"Dn{l}{t}")
                        wait_read(dve, f"Dn{l}{t}")
                    bk = wait_full(dve, f"Dt{l}{t}")
                    done(TT(DT[:, o], bk[:, :], DT[:, o], ALU.add), f"Dt{l}{t}")
                    wait_read(dve, f"Dt{l}{t}")
            wait_full(dve, f"Dt{len(LEVELS) - 1}1")
            tt(dsq, oatt, oatt, ALU.mult)
            V.tensor_reduce(ss, v3(dsq, 2), AX.X, ALU.add).then_inc(S["o_ss"], 1)
            dve.wait_ge(S["o_ss"], 1)
            for x in (0, 1):
                wait_read(dve, f"val{x}")
            for n in range(4):
                t, r = n // 2, C * (n % 2)
                rows = slice(r, r + C)
                o = slice(t * 512, (t + 1) * 512)
                if n == 0:
                    V.tensor_copy(VN[rows, o], VAL[rows, o]).then_inc(S["vn_new"], 1)
                else:
                    bk = wait_full(dve, f"vp{n}")
                    TT(VN[rows, o], VAL[rows, o], bk[rows, :], ALU.subtract).then_inc(S["vn_new"], 1)
                    dve.wait_ge(S["vn_new"], n + 1)
                    dve.sem_inc(read[where[f"vp{n}"][0]], 1)
                if n < 3:
                    bk = wait_full(dve, f"sn{n}")
                    if n == 0:
                        step(V.tensor_copy(ST, bk[:, :]))
                    else:
                        wait_full(dve, f"do{n}")
                        for h in range(DH):
                            hs = slice(h * P, (h + 1) * P)
                            step(STT(ST[:, hs], ST[:, hs], ecd[:, 8 * (n % 2) + 4 * t + h:8 * (n % 2) + 4 * t + h + 1],
                                     bk[:, hs], ALU.mult, ALU.add))
                    dve.sem_inc(S["s_new"], 1)
                    dve.sem_inc(read[where[f"sn{n}"][0]], 1)
            for n in range(4):
                wait_read(dve, f"do{n}")
            tt(dsq, odn, odn, ALU.mult)
            V.tensor_reduce(n_ss[:, 0:8], v3(dsq, 8), AX.X, ALU.add).then_inc(S["o_ss"], 1)
            for x in range(3):
                bk = wait_full(dve, f"mc{x}")
                done(TT(modc[:, 16 * x:16 * x + 16], v3(bk[:, :], 16)[:, :, 0], col("bada", 16 * x, 16), ALU.add), f"mc{x}")
                wait_read(dve, f"mc{x}")
            step(STT(sc1, modc[:, 8:16], 1.0, col("nmix", 0, 8), ALU.add, ALU.mult))
            step(STT(sc2, modc[:, 32:40], 1.0, col("nffn", 0, 8), ALU.add, ALU.mult))
            dve.wait_ge(S["o_rs"], 1)
            tt(v3(odn, 8), v3(odn, 8), bc(n_rs[:, 0:8], P), ALU.mult)
            tt(tok3[:, :, 512:1024], v3(odn, 2), v3(gate, 2), ALU.mult)
            TT(tok3[:, :, 0:512], v3(oatt, 2), bc(rstd, 512), ALU.mult).then_inc(S["o_tok"], 1)
            evac_T("oT")
            for i in range(F1, F1 + NH):
                w_rest(i)

            def add_x(name, c, t, sem):
                bk = wait_full(dve, name)
                xs = X3[:, t, c * 512:(c + 1) * 512]
                TT(xs, bk[:, :], xs, ALU.add).then_inc(S[sem], 1)
                return bk

            for c in range(2):
                for t in range(T):
                    add_x(f"mo{c}{t}", c, t, "x1_new")
                    dve.wait_ge(S["x1_new"], 2 * c + t + 1)
                    dve.sem_inc(read[where[f"mo{c}{t}"][0]], 1)
            norm_tok("n2")
            evac_T("n2T")
            for c in range(16):
                w_rest(F1 + c + NH)
                wait_read(dve, f"z{c}")
                z, z2 = zr[:, (c % 2) * 512:(c % 2 + 1) * 512], slice(2 * c, 2 * c + 2)
                tt(zf, z, z, ALU.mult)
                step(TS(zTR[:, z2, :], v3(zf, 2), 1.0, None, ALU.mult))
                TT(zTLR[:, z2, :], v3(zf, 2), zTR[:, z2, :].bitcast(fp32), ALU.subtract).then_inc(S["z_done"], 1)
                dve.wait_ge(S["z_done"], c + 1)
            for i in range(F1 + 16 + NH, W2 + 2):
                w_rest(i)
            for j in range(4):
                add_x(f"y{j}", j % 2, j // 2, "x2_new")
                dve.wait_ge(S["x2_new"], j + 1)
                dve.sem_inc(read[where[f"y{j}"][0]], 1)
            norm_tok("n3")
            evac_T("n3T")
            w_rest(W2 + 2)
            ROPE = {0: 0, 1: 1, 6: 2, 7: 3, 8: 4, 9: 5}
            dve.wait_ge(S["ang_done"], 1)
            for c in range(16):
                if 2 * c + 3 < 32:
                    w_rest(W2 + 2 * c + 3)
                for t in range(T):
                    n = f"p{c}_{t}"
                    o = t * 1024 + (c % 2) * 512
                    if c in ROPE:
                        x = ROPE[c]
                        bk = wait_full(dve, n)
                        cos, sin = cosin[:, t * 64:(t + 1) * 64], cosin[:, 128 + t * 64:128 + (t + 1) * 64]
                        step(TT(v3(ropeA, 8), v3(bk[:, :], 8), bm(cos, 8), ALU.mult))
                        done(TT(v3(ropeB, 8), v3(bk[:, :], 8), bm(sin, 8), ALU.mult), n)
                        wait_read(dve, n)
                        A4, B4 = (r.rearrange("p (h a n) -> p h a n", h=4, a=2) for r in (ropeA, ropeB))
                        O4 = ropeO[:, t * 512:(t + 1) * 512].rearrange("p (h a n) -> p h a n", h=4, a=2)
                        if x:
                            wait_full(dve, f"rT{x - 1}{t}")
                        if x == 2 and t == 0:
                            dve.wait_ge(S["kz_done"], 1)
                        tt(O4[:, :, 0, :], A4[:, :, 0, :], B4[:, :, 1, :], ALU.subtract)
                        TT(O4[:, :, 1, :], A4[:, :, 1, :], B4[:, :, 0, :], ALU.add).then_inc(S["rope_out"], 1)
                        dve.wait_ge(S["rope_out"], 2 * x + t + 1)
                        if x == 1 and t == 0:
                            TT(v3(KZ, 4), v3(ropeO[:, 0:512], 4), bc(K("zeta"), P), ALU.mult).then_inc(S["kz_done"], 1)
                    elif c in (4, 5):
                        i = 2 * (c - 4) + t
                        dve.wait_ge(S["g_exp"], i + 1)
                        gx = gex[:, t * 512:(t + 1) * 512]
                        TT(RG[:, o:o + 512], RG[:, o:o + 512], gx, ALU.mult).then_inc(S["gate2"], 1)
                        dve.wait_ge(S["gate2"], i + 1)
                    elif c >= 12:
                        wait_read(dve, n)
                if 2 * c + 4 < 32:
                    w_rest(W2 + 2 * c + 4)

            for t in range(T):
                bk = wait_full(dve, f"rs{t}")
                TT(sT[:, t * 512:(t + 1) * 512], bk[:, :], K("dmaskT"), ALU.mult).then_inc(S["st_done"], 1)
                dve.wait_ge(S["st_done"], t + 1)
                dve.sem_inc(read[where[f"rs{t}"][0]], 1)
            for hh in range(2):
                wait_read(dve, f"ro1{hh}")
                bk = wait_full(dve, f"rx{hh}")
                for h in range(2):
                    hd = 2 * hh + h
                    o = tok[:, 1024 + hd * 256:1024 + (hd + 1) * 256]
                    i = STT(o, bk[:, h * 256:(h + 1) * 256], K("xi")[:, hd:hd + 1], o, ALU.mult, ALU.add)
                done(i, f"rx{hh}")
                wait_read(dve, f"rx{hh}")

            def head_norm(i):
                tt(sq2, tok[:, :], tok[:, :], ALU.mult)
                V.tensor_reduce(n_ss[:, 0:8], v3(sq2, 8), AX.X, ALU.add).then_inc(S["head_ss"], 1)
                dve.wait_ge(S["head_rs"], i + 1)

            for hh in range(2):
                wait_read(dve, f"ro0{hh}")
            head_norm(0)
            tt(v3(tok[:, :], 8), v3(tok[:, :], 8), bc(n_rs[:, 0:8], RV), ALU.mult)
            for t in range(T):
                TT(tok3[:, t, :], tok3[:, t, :], RG[:, t * 1024:(t + 1) * 1024], ALU.mult).then_inc(S["r_tok"], 1)
            for x in range(8):
                bk = wait_full(dve, f"ps{x}")
                step(V.tensor_reduce(a_mx[:, 2 * x:2 * x + 1], bk[:, 0:P], AX.X, ALU.max, negate=True))
                step(V.tensor_reduce(a_mx[:, 2 * x + 1:2 * x + 2], bk[:, P:384], AX.X, ALU.max, negate=True))
                TS(a_mx[:, 2 * x:2 * x + 2], a_mx[:, 2 * x:2 * x + 2], RK ** -0.5, None, ALU.mult)\
                    .then_inc(S["p_max"], 1)
            dve.wait_ge(S["p_exp"], 8)
            evac_T("rtT")
            wait_read(dve, "lam")
            step(STT(lam, lame[:, 0:1], LAMI, lame[:, 1:2], ALU.add, ALU.subtract))
            step(V.reciprocal(a_rd, a_sum))
            a4v = a_rd.rearrange("p (h c t) -> p h c t", h=4, c=2)
            step(TS(a4v[:, :, 1, :], a4v[:, :, 1, :], lam, None, ALU.mult))
            for h in range(RH):
                for r in range(2):
                    w = slice(0, P) if r == 0 else slice(P, 384)
                    j = 4 * h + r
                    step(TS(P2[:, 2 * h + 1, w], P2[:, 2 * h + 1, w], a_rd[:, j + 2:j + 3], None, ALU.mult))
                    i = STT(P2[:, 2 * h, w], P2[:, 2 * h, w], a_rd[:, j:j + 1], P2[:, 2 * h + 1, w], ALU.mult, ALU.subtract)
                    if r == 0:
                        step(i)
                i.then_inc(S["a_done"], 1)
            for c in range(2):
                for t in range(T):
                    n = f"rp{c}{t}"
                    bk = wait_full(dve, n)
                    o = slice(t * 1024 + c * 512, t * 1024 + (c + 1) * 512)
                    done(TT(GR[:, o], bk[:, :], GR[:, o], ALU.mult), n)
            for h in range(1, RH, 2):
                bk = wait_full(dve, f"pT{h}")
                done(V.tensor_copy(PT2[:, h, :], bk[:, 0:384]), f"pT{h}")
            for t in range(T):
                for hh in range(2):
                    wait_read(dve, f"po{t}{hh}")
            head_norm(1)
            for t in range(T):
                TT(v3(tok3[:, t, :], 4), v3(tok3[:, t, :], 4), bc(n_rs[:, 4 * t:4 * t + 4], RV), ALU.mult)\
                    .then_inc(S["r_tok"], 1)
            evac_T("dtT")
            step(TT(v3(gdiag[:, 0:1024], 8), bm(ident, 8), bc(modc[:, 16:24], P), ALU.mult))
            TT(v3(gdiag[:, 1024:2048], 8), bm(ident, 8), bc(modc[:, 40:48], P), ALU.mult).then_inc(S["diag"], 1)
            for c in range(2):
                for t in range(T):
                    n = f"wd{c}{t}"
                    bk = wait_full(dve, n)
                    o = slice(t * 1024 + c * 512, t * 1024 + (c + 1) * 512)
                    done(TT(GD[:, o], bk[:, :], GD[:, o], ALU.mult), n)
                    wait_read(dve, n)
                    i = TT(GR[:, o], GR[:, o], GD[:, o], ALU.add)
            i.then_inc(S["m_done"], 1)
            evac_T("mT")
            for x in range(4):
                wait_read(dve, f"gr{x}")
            for c in range(2):
                for t in range(T):
                    n = f"xo{c}{t}"
                    bk = wait_full(dve, n)
                    o = tok3[:, t, c * 512:(c + 1) * 512]
                    xs = X3[:, t, c * 512:(c + 1) * 512]
                    done(TT(o, bk[:, :], grow1[:, c * 512:(c + 1) * 512], ALU.mult), n)
                    wait_read(dve, n)
                    TT(xs, xs, o, ALU.add).then_inc(S["x3_new"], 1)
            norm_tok("n4")
            evac_T("n4T")
            bk = wait_full(dve, "rout")
            done(TT(v3(lg[:, :], 2), v3(bk[:, 0:72], 2), bm(rbias, 2), ALU.add), "rout")
            wait_read(dve, "rout")
            l2 = v3(lg[:, :], 2)
            G, EL = l2[:, :, 0:4], l2[:, :, 4:36]
            gm, gs, gtop, m1, m2, w1, w2 = (rs8[:, 2 * i:2 * i + 2] for i in (0, 1, 2, 3, 5, 6, 7))
            e2 = rs8[:, 8:10]
            r4, hot4 = v3(rt[:, 0:8], 2), v3(rt[:, 8:16], 2)
            pr4 = K("prio")[:, 28:32]
            step(V.tensor_reduce(gm, G, AX.X, ALU.max))
            TT(r4, G, bc(gm, 4), ALU.subtract).then_inc(S["router_req"], 1)
            tt(hot4, G, bc(gm, 4), ALU.is_equal)
            tt(hot4, hot4, bm(pr4, 2), ALU.mult)
            step(V.tensor_reduce(m1, hot4, AX.X, ALU.max))
            tt(hot4, hot4, bc(m1, 4), ALU.is_equal)
            step(TS(hot4, hot4, -1.0, -NEG, ALU.add, ALU.mult))
            mel = rt2[:, 0:64]
            step(V.tensor_copy(v3(mel, 2), EL))
            tt(v3(mel, 8), v3(mel, 8), bc(rt[:, 8:16], EG), ALU.add)
            h1, h2 = v3(rt3[:, 0:64], 2), v3(Wt[:, :], 2)

            def first_best(h, m):
                step(V.tensor_reduce(m, v3(mel, 2), AX.X, ALU.max))
                tt(h, v3(mel, 2), bc(m, E), ALU.is_equal)
                tt(h, h, bm(K("prio"), 2), ALU.mult)
                step(V.tensor_reduce(gm, h, AX.X, ALU.max))
                tt(h, h, bc(gm, E), ALU.is_equal)

            first_best(h1, m1)
            step(STT(mel, rt3[:, 0:64], 3 * NEG, mel, ALU.mult, ALU.add))
            first_best(h2, m2)
            TT(e2, m2, m1, ALU.subtract).then_inc(S["router_req"], 1)
            dve.wait_ge(S["router_exp"], 2)
            step(V.tensor_reduce(gs, r4, AX.X, ALU.add))
            step(V.reciprocal(gtop, gs))
            step(TS(w1, e2, 1.0, None, ALU.add))
            step(V.reciprocal(w1, w1))
            tt(w1, w1, gtop, ALU.mult)
            tt(w2, w1, e2, ALU.mult)
            TT(v3(sel, 2), h1, h2, ALU.add).then_inc(S["sel_ready"], 1)
            dve.wait_ge(S["sel_ready"], 1)
            tt(h1, h1, bc(w1, E), ALU.mult)
            tt(h2, h2, bc(w2, E), ALU.mult)
            step(V.memset(RW, -1.0))
            RW3 = RW.rearrange("p (e c) -> p c e", c=4)
            tt(RW3[:, 2:4, 0:E], h2, h1, ALU.add)
            for b in (PT[0][0], PT[0][1], PT[1][0], PT[1][1], ysb, ZT[0]):
                step(V.memset(b, 0.0))
            dve.sem_inc(S["moe_zero"], 1)
            bk = wait_full(dve, "rank")
            step(V.tensor_copy(cnt, bk[:, 64:96]))
            step(STT(v3(rt2[:, 0:64], 2), v3(bk[:, 0:64], 2), 1024.0, v3(sel, 2), ALU.add, ALU.mult))
            done(TS(RW3[:, 0:2, 0:E], v3(rt2[:, 0:64], 2), -1024.0, None, ALU.add), "rank")
            wait_read(dve, "rank")
            step(V.tensor_reduce(flagf[:, 0:1], cnt, AX.X, ALU.max))
            step(TS(flagf[:, 0:1], flagf[:, 0:1], float(CAP), None, ALU.is_gt))
            V.tensor_copy(flagi[:, 0:1], flagf[:, 0:1]).then_inc(S["flag_ready"], 1)

            def place_slots(pw, sem):
                for t in range(T):
                    TS(Pm[:, t * SL:(t + 1) * SL], iota, cur[:, t:t + 1], None, ALU.is_equal)
                for t in range(T):
                    for j in range(2):
                        o = (2 * t + j) * SL
                        i = TS(pw[:, o:o + SL], iota, cur[:, t:t + 1], cur[:, 2 + t:3 + t], ALU.is_equal, ALU.mult)
                i.then_inc(sem, 1)

            def silu_mult(link, sem):
                link(TT(gex2, banks[BG][:, 0:256], gex2, ALU.mult))
                TT(hid, banks[BG][:, 256:512], gex2, ALU.mult).then_inc(sem, 1)

            iota = K("iota")[:, 0:SL]
            step(V.tensor_copy(cur, RW[:, 0:4]))
            place_slots(PwD[0], S["p_ready"])
            dve.sem_inc(S["moe_hid"], 1)
            with dve.Fori(0, E // 2) as it:
                for u in range(2):
                    local = [0]

                    def link(ins):
                        local[0] += 1
                        ins.then_inc(S["hid_step"], 1)
                        dve.wait_ge(S["hid_step"], 4 * it + (2 * u + local[0]))

                    dve.wait_ge(full[BX], base[BX] + 2 * it + (u + 1))
                    dve.wait_ge(S["p_ready"], 2 * it + (u + 1))
                    dve.wait_ge(full[BH], base[BH] + 2 * it + u)
                    link(TS(cur, RW[:, bass.ds(8 * it + 4 * (u + 1), 4)], 1.0, None, ALU.mult))
                    place_slots(PwD[1 - u], S["p_ready"])
                    dve.wait_ge(S["moe_exp"], 2 * it + (u + 1))
                    silu_mult(link, S["moe_hid"])
                    dve.wait_ge(S["moe_hid"], 2 * it + (u + 2))
            over = dve.value_load(flagi[0:1, 0:1], min_val=0, max_val=1)
            with dve.If(over > 0):
                dve.wait_ge(S["over_go"], 1)
                with dve.Fori(0, E) as e:
                    for k in range(NOVER):
                        local = [0]

                        def link(ins):
                            local[0] += 1
                            ins.then_inc(S["over_step"], 1)
                            dve.wait_ge(S["over_step"], 3 * NOVER * e + (3 * k + local[0]))

                        if k:
                            dve.wait_ge(S["over_sc"], NOVER * e + k)
                        link(TS(cur, RW[:, bass.ds(4 * e, 4)], 1.0, None, ALU.mult))
                        link(TS(cur[:, 0:2], cur[:, 0:2], -float(CAP + SL * k), None, ALU.add))
                        place_slots(PwD[0], S["over_p"])
                        dve.wait_ge(S["over_e"], NOVER * e + (k + 1))
                        silu_mult(link, S["over_a"])
                        dve.wait_ge(S["over_a"], NOVER * e + (k + 1))
                    dve.wait_ge(S["over_sc"], NOVER * e + NOVER)
                    dve.sem_inc(S["over_go"], 1)
            dve.wait_ge(S["y_sum"], 1)
            for t in range(T):
                for hh in range(2):
                    ys = scaled[:, t * 1024 + hh * 512:t * 1024 + (hh + 1) * 512]
                    step(TT(ys, banks[4 + 2 * t + hh][:, :], G2[:, hh * 512:(hh + 1) * 512], ALU.mult))
                i = TT(X3[:, t, :], X3[:, t, :], scaled[:, t * 1024:(t + 1) * 1024], ALU.add)
            i.then_inc(S["y_done"], 1)
            dve.wait_ge(S["n5_rs"], 1)
            dve.wait_ge(S["fin_in"], 16)
            for t in range(T):
                step(TS(tok3[:, t, :], X3[:, t, :], rstd[:, t:t + 1], None, ALU.mult))
                i = TT(tok3[:, t, :], tok3[:, t, :], fing, ALU.mult)
                if t == 0:
                    step(i)
            i.then_inc(S["out_done"], 1)

        @block.gpsimd
        def _(pool):
            def row_in(dst, src, sem):
                pool.dma_start(dst, src.to_broadcast([P, src.shape[1]])).then_inc(S[sem], 16)

            pool.dma_start(posi[:, :], g["positions_2"].rearrange("o (t p) -> p (o t)", p=P),
                           allow_slow_non_contiguous=True).then_inc(S["pos_in"], 16)
            row_in(dtb, g["dn_dt_bias"], "vec_in")
            row_in(alog, g["dn_a_log"], "vec_in")
            row_in(rbias[:, 0:4], g["b_router_group_2"], "vec_in")
            row_in(rbias[:, 4:36], g["b_router_expert_2"], "vec_in")
            nc.gpsimd.memset(cin[:, :, 0:3], 0.0).then_inc(S["cin_zero"], 1)
            rb = g["rel_bias"]
            for h in range(AH):
                for kt in range(2):
                    n = 256 if kt == 0 else P
                    src = bass.AP(rb.tensor, h * NREL + MAXREL - P + 1, [[1, P], [1, n]])
                    pool.dma_start(bias[:, h, kt * 256:kt * 256 + n], src).then_inc(S["bias_in"], 16)
            pool.wait_ge(S["bias_in"], 16 * 2 * AH)
            nc.gpsimd.memset(bias[0:C, :, 0:C], NEG).then_inc(S["pool_step"], 1)
            pool.wait_ge(S["pool_step"], 1)
            nc.gpsimd.memset(bias[0:C, :, 256:256 + C], NEG).then_inc(S["bias_masked"], 1)
            for l, s in enumerate(LEVELS):
                for t in range(T):
                    o = slice(t * 512, (t + 1) * 512)
                    if l == 0:
                        wait_read(pool, f"kk0{t}")
                    else:
                        wait_full(pool, f"Y{l - 1}{t}")
                    nc.gpsimd.tensor_tensor(v3(AM[:, o], 4), v3(AT[:, o], 4), bm(K(f"lvl{s}"), 4), ALU.mult)\
                        .then_inc(S["am_ready"], 1)
            pool.wait_ge(S["diag"], 1)
            pool.dma_start(wr[:, :, 0:4], g["w_router_group_2"][0].rearrange("(k p) n -> p k n", p=P)).then_inc(S["wr_in"], 16)
            pool.dma_start(wr[:, :, 4:36], g["w_router_expert_2"][0].rearrange("(k p) n -> p k n", p=P)).then_inc(S["wr_in"], 16)
            row_in(fing, g["norm_final_2"].rearrange("(o n) -> o n", o=1), "fin_in")
            pool.wait_ge(S["fin_in"], 16)
            pool.wait_ge(S["wr_in"], 32)

        @block.sync
        def _(sp):
            def src_of(kind, c):
                w = wsrc[kind][0]
                if kind == "ff2":
                    return w[c * 512:(c + 1) * 512, :].rearrange("(k p) n -> p k n", p=P)
                cols = min(WC, w.shape[1] - c * WC)
                return w[:, c * WC:c * WC + cols].rearrange("(k p) n -> p k n", p=P)

            for t in range(T):
                sp.dma_start(X3[:, t, :], g["x"][0, t * P:(t + 1) * P, :]).then_inc(S["x_in"], 16)
            for n, (kind, c) in enumerate(order):
                if n == 1:
                    sp.wait_ge(S["x_in"], 32)
                    sp.wait_ge(S["const_in"], 16)
                    sp.wait_ge(S["rows_in"], 16 * NROWS)
                if n >= NR:
                    k0, c0 = order[n - NR]
                    if k0 == "ff2" and c0 < 7:
                        sp.wait_ge(S["ff2_used"], c0 + 1)
                    else:
                        wait_full(sp, last_job[n - NR])
                src = src_of(kind, c)
                sp.dma_start(weights(kind, c)[:, :, 0:src.shape[2]], src).then_inc(w_in[n % NR], 16)

            exps = (g["w_exp_gate_2"][0], g["w_exp_up_2"][0], g["w_exp_down_2"][0])

            def expert_load(s, e):
                m = s % 3
                w = exps[m]
                src = w[bass.ds(e, 1), :, :].rearrange("o (k p) n -> p (o k) n", p=P)
                ins = sp.dma_start(v3(mslot(s), 4 if m == 2 else KT), src)
                ins.then_inc(w_in[s] if s < NR else wx_in[s - NR], 16)

            for s in range(6):
                if s < NR:
                    wait_full(sp, last_job[NW - NR + s])
                else:
                    sp.wait_ge(S["n4_tok"], 2)
                expert_load(s, s // 3)
            with sp.Fori(0, E // 2 - 1) as it:
                for s in range(6):
                    u, m = s // 3, s % 3
                    b = BO if m == 2 else BG
                    sp.wait_ge(full[b], base[b] + 2 * it + (u + 1))
                    expert_load(s, 2 * it + (u + 2))
            sp.wait_ge(S["flag_ready"], 1)
            over = sp.value_load(flagi[0:1, 0:1], min_val=0, max_val=1)
            with sp.If(over > 0):
                with sp.Fori(0, E) as e:
                    sp.wait_ge(S["over_go"], e + 1)
                    for m in range(3):
                        src = exps[m][bass.ds(e, 1), :, :].rearrange("o (k p) n -> p (o k) n", p=P)
                        sp.dma_start(v3(mslot(m), 4 if m == 2 else KT), src).then_inc(S["over_w"], 16)


_INS = ("x mix_norm_gain w_in att_q_gain att_k_gain rel_bias att_out_gain dn_conv_w dn_a_log dn_dt_bias dn_out_gain "
        "w_out ffn_norm_gain w_ff1 w_ff2 c_2 positions_2 w_ada_2 b_ada_2 norm_mix_2 w_in_2 w_ret_o_2 w_diff_o_2 "
        "lam_q1_2 lam_k1_2 lam_q2_2 lam_k2_2 diff_norm_2 w_out_2 norm_ffn_2 w_router_group_2 b_router_group_2 "
        "w_router_expert_2 b_router_expert_2 w_exp_gate_2 w_exp_up_2 w_exp_down_2 norm_final_2").split()


def kernel(**inputs):
    import numpy as _np
    import concourse.bacc as _bacc
    from concourse import mybir as _mybir
    from concourse.bass_utils import run_bass_kernel_spmd as _run

    nc = _bacc.Bacc("TRN2", target_bir_lowering=False, num_devices=1)
    arrays, g = {}, {}
    for name in _INS:
        a = _np.ascontiguousarray(inputs[name])
        arrays[f"in_{name}"] = a
        g[name] = nc.dram_tensor(f"in_{name}", a.shape, _mybir.dt.from_np(a.dtype), kind="ExternalInput").ap()
    a = constants()
    arrays["in_const"] = a
    g["const"] = nc.dram_tensor("in_const", a.shape, _mybir.dt.from_np(a.dtype), kind="ExternalInput").ap()
    out = nc.dram_tensor("out_0", (1, T * P, D), _mybir.dt.float32, kind="ExternalOutput").ap()
    program(nc, g, out)
    r = _run(nc, [arrays], core_ids=[0])
    return r.results[0]["out_0"]
```
